# Optimizing a Trainium2 kernel written in Bass

```python
import jax
import jax.numpy as jnp
from jax import lax
import numpy as np

D_MODEL = 1024
BATCH = 1
SEQ = 256
DEPTH = 2

N_A_LAYERS = DEPTH // 2
N_B_LAYERS = DEPTH - N_A_LAYERS
N_HEADS = 8
HEAD_DIM = D_MODEL // N_HEADS
N_KV_HEADS = 2
HEAD_GROUP = N_HEADS // N_KV_HEADS
KV_DIM = N_KV_HEADS * HEAD_DIM
IDX_HEADS = 4
IDX_DIM = 64
IDX_TOPK_MAX = 256
DSA_Q_BLOCK = 128
MOBA_BLOCK = 256
MOBA_TOPK = 3
MOBA_Q_CHUNK = 16
N_GROUPS = 4
EXPERTS_PER_GROUP = 8
N_EXPERTS = N_GROUPS * EXPERTS_PER_GROUP
TOP_EXPERTS = 2
D_EXPERT = 512
MOE_ROW_BLOCK = 128
PLE_DIM = 256
ALPHA = (2.0 * DEPTH) ** 0.25
BETA = (8.0 * DEPTH) ** -0.25
LN_EPS = 1e-5
A_SPLITS = (D_MODEL, D_MODEL + KV_DIM, D_MODEL + 2 * KV_DIM,
            D_MODEL + 2 * KV_DIM + IDX_HEADS * IDX_DIM,
            D_MODEL + 2 * KV_DIM + IDX_HEADS * IDX_DIM + IDX_DIM)
A_COLS = A_SPLITS[-1] + IDX_HEADS

kernel_name = 'yoco_dsa_moba_hmoe_trunk'

def alibi_slopes(n):
    return 2.0 ** (-8.0 * jnp.arange(1, n + 1, dtype=jnp.float32) / n)

def layer_norm(x, g, b):
    xf = x.astype(jnp.float32)
    mu = jnp.mean(xf, axis=-1, keepdims=True)
    var = jnp.mean(jnp.square(xf - mu), axis=-1, keepdims=True)
    y = (xf - mu) * lax.rsqrt(var + LN_EPS) * g.astype(jnp.float32) + b.astype(jnp.float32)
    return y.astype(x.dtype)

def dsa_attention(h, w_in, w_o, slopes):
    bsz, seq, _ = h.shape
    q, k, v, iq, ik, iw = jnp.split(h @ w_in, A_SPLITS, axis=-1)
    q = q.reshape(bsz, seq, N_KV_HEADS, HEAD_GROUP, HEAD_DIM)
    k = k.reshape(bsz, seq, N_KV_HEADS, HEAD_DIM)
    v = v.reshape(bsz, seq, N_KV_HEADS, HEAD_DIM)
    iq = iq.reshape(bsz, seq, IDX_HEADS, IDX_DIM)
    iw = iw * (IDX_HEADS ** -0.5)
    topk = min(IDX_TOPK_MAX, seq // 4)
    n_blk = seq // DSA_Q_BLOCK
    key_pos = jnp.arange(seq)
    b_ix = jnp.arange(bsz)[:, None, None]
    slope = slopes.reshape(N_KV_HEADS, HEAD_GROUP)[None, None, :, :, None]

    def block(i):
        start = i * DSA_Q_BLOCK
        qb = lax.dynamic_slice_in_dim(q, start, DSA_Q_BLOCK, axis=1)
        iqb = lax.dynamic_slice_in_dim(iq, start, DSA_Q_BLOCK, axis=1)
        iwb = lax.dynamic_slice_in_dim(iw, start, DSA_Q_BLOCK, axis=1)
        qpos = start + jnp.arange(DSA_Q_BLOCK)
        rel = jax.nn.relu(jnp.einsum('bqhd,bsd->bqhs', iqb, ik) * (IDX_DIM ** -0.5))
        score = jnp.einsum('bqhs,bqh->bqs', rel, iwb).astype(jnp.float32)
        score = jnp.where(key_pos[None, None, :] <= qpos[None, :, None], score, -jnp.inf)
        _, idx = lax.top_k(score, topk)
        kg = k[b_ix, idx]
        vg = v[b_ix, idx]
        logits = jnp.einsum('bqgrd,bqkgd->bqgrk', qb, kg).astype(jnp.float32) * (HEAD_DIM ** -0.5)
        dist = (qpos[None, :, None] - idx).astype(jnp.float32)[:, :, None, None, :]
        logits = logits - slope * dist
        valid = (idx <= qpos[None, :, None])[:, :, None, None, :]
        probs = jax.nn.softmax(jnp.where(valid, logits, -jnp.inf), axis=-1).astype(v.dtype)
        out = jnp.einsum('bqgrk,bqkgd->bqgrd', probs, vg)
        return out.reshape(bsz, DSA_Q_BLOCK, D_MODEL)

    out = lax.map(block, jnp.arange(n_blk))
    out = out.transpose(1, 0, 2, 3).reshape(bsz, seq, D_MODEL)
    return out @ w_o

def shared_block_kv(h, w_kv):
    bsz, seq, _ = h.shape
    k, v = jnp.split(h @ w_kv, 2, axis=-1)
    n_blocks = -(-seq // MOBA_BLOCK)
    pad = n_blocks * MOBA_BLOCK - seq

    def to_blocks(t):
        t = jnp.pad(t, ((0, 0), (0, pad), (0, 0)))
        return t.reshape(bsz, n_blocks, MOBA_BLOCK, N_KV_HEADS, HEAD_DIM).transpose(0, 3, 1, 2, 4)

    k_blocks = to_blocks(k)
    v_blocks = to_blocks(v)
    k_means = jnp.mean(k_blocks.astype(jnp.float32), axis=3).astype(h.dtype)
    return k_blocks, v_blocks, k_means

def moba_attention(h, w_q, w_o, k_blocks, v_blocks, k_means, slopes):
    bsz, seq, _ = h.shape
    n_blocks = k_blocks.shape[2]
    n_sel = max(1, min(MOBA_TOPK, n_blocks - 1))
    n_past_cols = n_sel * MOBA_BLOCK
    q = (h @ w_q).reshape(bsz, seq, N_KV_HEADS, HEAD_GROUP, HEAD_DIM)
    blk_ids = jnp.arange(n_blocks)
    in_blk = jnp.arange(MOBA_BLOCK)
    b_ix = jnp.arange(bsz)[:, None, None, None, None]
    g_ix = jnp.arange(N_KV_HEADS)[None, None, :, None, None]
    slope = slopes.reshape(N_KV_HEADS, HEAD_GROUP)[None, None, :, :, None]
    scale = HEAD_DIM ** -0.5

    def chunk(c):
        start = c * MOBA_Q_CHUNK
        qc = lax.dynamic_slice_in_dim(q, start, MOBA_Q_CHUNK, axis=1)
        qpos = start + jnp.arange(MOBA_Q_CHUNK)
        own = start // MOBA_BLOCK
        gate = jnp.einsum('bqgrd,bgnd->bqgrn', qc, k_means).astype(jnp.float32)
        gate = jnp.where(blk_ids < own, gate, -jnp.inf)
        _, sel = lax.top_k(gate, n_sel)
        ks = k_blocks[b_ix, g_ix, sel]
        vs = v_blocks[b_ix, g_ix, sel]
        ko = lax.dynamic_index_in_dim(k_blocks, own, axis=2, keepdims=False)
        vo = lax.dynamic_index_in_dim(v_blocks, own, axis=2, keepdims=False)
        past = jnp.einsum('bqgrd,bqgrjpd->bqgrjp', qc, ks).astype(jnp.float32) * scale
        kpos = sel[..., None] * MOBA_BLOCK + in_blk
        past_dist = (qpos[None, :, None, None, None, None] - kpos).astype(jnp.float32)
        past = past - slope[..., None] * past_dist
        past = jnp.where((sel < own)[..., None], past, -jnp.inf)
        past = past.reshape(bsz, MOBA_Q_CHUNK, N_KV_HEADS, HEAD_GROUP, n_past_cols)
        selfb = jnp.einsum('bqgrd,bgpd->bqgrp', qc, ko).astype(jnp.float32) * scale
        own_dist = (qpos[:, None] - (own * MOBA_BLOCK + in_blk)[None, :]).astype(jnp.float32)
        selfb = selfb - slope * own_dist[None, :, None, None, :]
        selfb = jnp.where((own_dist >= 0)[None, :, None, None, :], selfb, -jnp.inf)
        probs = jax.nn.softmax(jnp.concatenate([past, selfb], axis=-1), axis=-1).astype(v_blocks.dtype)
        p_past = probs[..., :n_past_cols].reshape(bsz, MOBA_Q_CHUNK, N_KV_HEADS, HEAD_GROUP, n_sel, MOBA_BLOCK)
        p_own = probs[..., n_past_cols:]
        out = (jnp.einsum('bqgrjp,bqgrjpd->bqgrd', p_past, vs)
               + jnp.einsum('bqgrp,bgpd->bqgrd', p_own, vo))
        return out.reshape(bsz, MOBA_Q_CHUNK, D_MODEL)

    out = lax.map(chunk, jnp.arange(seq // MOBA_Q_CHUNK))
    out = out.transpose(1, 0, 2, 3).reshape(bsz, seq, D_MODEL)
    return out @ w_o

def hier_moe(h, w_rg, b_rg, w_re, b_re, w_gate, w_up, w_down):
    bsz, seq, _ = h.shape
    n_tok = bsz * seq
    n_assign = n_tok * TOP_EXPERTS
    xt = h.reshape(n_tok, D_MODEL)
    g_logits = (xt @ w_rg + b_rg).astype(jnp.float32)
    g_prob = jax.nn.softmax(g_logits, axis=-1)
    g_sel = jnp.argmax(g_logits, axis=-1)
    g_w = jnp.take_along_axis(g_prob, g_sel[:, None], axis=-1)
    e_logits = (xt @ w_re + b_re).astype(jnp.float32).reshape(n_tok, N_GROUPS, EXPERTS_PER_GROUP)
    e_logits = jnp.take_along_axis(e_logits, g_sel[:, None, None], axis=1)[:, 0]
    e_val, e_loc = lax.top_k(e_logits, TOP_EXPERTS)
    e_w = jax.nn.softmax(e_val, axis=-1) * g_w
    e_id = g_sel[:, None] * EXPERTS_PER_GROUP + e_loc
    flat_e = e_id.reshape(-1)
    flat_tok = jnp.repeat(jnp.arange(n_tok), TOP_EXPERTS)
    flat_w = e_w.reshape(-1)
    order = jnp.argsort(flat_e)
    se, stok, sw = flat_e[order], flat_tok[order], flat_w[order]
    counts = jnp.bincount(flat_e, length=N_EXPERTS)
    padded = (counts + MOE_ROW_BLOCK - 1) // MOE_ROW_BLOCK * MOE_ROW_BLOCK
    pad_end = jnp.cumsum(padded)
    pad_start = pad_end - padded
    raw_start = jnp.cumsum(counts) - counts
    dest = pad_start[se] + (jnp.arange(n_assign) - raw_start[se])
    n_rows = (n_assign + N_EXPERTS * (MOE_ROW_BLOCK - 1) + MOE_ROW_BLOCK - 1) // MOE_ROW_BLOCK * MOE_ROW_BLOCK
    n_row_blocks = n_rows // MOE_ROW_BLOCK
    rows = jnp.zeros((n_rows, D_MODEL), h.dtype).at[dest].set(xt[stok])
    blk_expert = jnp.minimum(
        jnp.searchsorted(pad_end, jnp.arange(n_row_blocks) * MOE_ROW_BLOCK, side='right'),
        N_EXPERTS - 1)

    def expert_block(args):
        xb, e = args
        return (jax.nn.silu(xb @ w_gate[e]) * (xb @ w_up[e])) @ w_down[e]

    yb = lax.map(expert_block, (rows.reshape(n_row_blocks, MOE_ROW_BLOCK, D_MODEL), blk_expert))
    y = yb.reshape(n_rows, D_MODEL)[dest] * sw[:, None].astype(h.dtype)
    out = jax.ops.segment_sum(y, stok, num_segments=n_tok)
    return out.reshape(bsz, seq, D_MODEL)

def setup_inputs(seed: int = 0) -> dict:
    key = jax.random.key(seed)
    ks = jax.random.split(key, 18)
    f32 = jnp.float32

    def nrm(k, shape, scale):
        return jax.random.normal(k, shape, f32) * scale

    a_col_scale = jnp.concatenate([
        jnp.ones((D_MODEL + KV_DIM,), f32),
        jnp.full((KV_DIM,), BETA, f32),
        jnp.ones((A_COLS - D_MODEL - 2 * KV_DIM,), f32)])
    kv_col_scale = jnp.concatenate([jnp.ones((KV_DIM,), f32), jnp.full((KV_DIM,), BETA, f32)])
    return {
        'x': nrm(ks[0], (BATCH, SEQ, D_MODEL), 1.0),
        'p': nrm(ks[1], (DEPTH, BATCH, SEQ, PLE_DIM), 1.0),
        'w_in_a': nrm(ks[2], (N_A_LAYERS, D_MODEL, A_COLS), D_MODEL ** -0.5) * a_col_scale,
        'w_o_a': nrm(ks[3], (N_A_LAYERS, D_MODEL, D_MODEL), BETA * D_MODEL ** -0.5),
        'w_kv_shared': nrm(ks[4], (D_MODEL, 2 * KV_DIM), D_MODEL ** -0.5) * kv_col_scale,
        'w_q_b': nrm(ks[5], (N_B_LAYERS, D_MODEL, D_MODEL), D_MODEL ** -0.5),
        'w_o_b': nrm(ks[6], (N_B_LAYERS, D_MODEL, D_MODEL), BETA * D_MODEL ** -0.5),
        'w_router_group': nrm(ks[7], (DEPTH, D_MODEL, N_GROUPS), D_MODEL ** -0.5),
        'b_router_group': nrm(ks[8], (DEPTH, N_GROUPS), 0.01),
        'w_router_expert': nrm(ks[9], (DEPTH, D_MODEL, N_EXPERTS), D_MODEL ** -0.5),
        'b_router_expert': nrm(ks[10], (DEPTH, N_EXPERTS), 0.01),
        'w_gate': nrm(ks[11], (DEPTH, N_EXPERTS, D_MODEL, D_EXPERT), D_MODEL ** -0.5),
        'w_up': nrm(ks[12], (DEPTH, N_EXPERTS, D_MODEL, D_EXPERT), D_MODEL ** -0.5),
        'w_down': nrm(ks[13], (DEPTH, N_EXPERTS, D_EXPERT, D_MODEL), BETA * D_EXPERT ** -0.5),
        'w_ple': nrm(ks[14], (DEPTH, PLE_DIM, D_MODEL), BETA * PLE_DIM ** -0.5),
        'w_ple_gate': nrm(ks[15], (DEPTH, D_MODEL, D_MODEL), D_MODEL ** -0.5),
        'ln_g': 1.0 + nrm(ks[16], (DEPTH, 3, D_MODEL), 0.02),
        'ln_b': nrm(ks[17], (DEPTH, 3, D_MODEL), 0.02),
    }

def reference(x, p, w_in_a, w_o_a, w_kv_shared, w_q_b, w_o_b, w_router_group, b_router_group,
              w_router_expert, b_router_expert, w_gate, w_up, w_down, w_ple, w_ple_gate, ln_g, ln_b):
    slopes = alibi_slopes(N_HEADS)
    h = x
    for i in range(DEPTH):
        if i < N_A_LAYERS:
            mix = dsa_attention(h, w_in_a[i], w_o_a[i], slopes)
        else:
            if i == N_A_LAYERS:
                k_blocks, v_blocks, k_means = shared_block_kv(h, w_kv_shared)
            j = i - N_A_LAYERS
            mix = moba_attention(h, w_q_b[j], w_o_b[j], k_blocks, v_blocks, k_means, slopes)
        h = layer_norm(ALPHA * h + mix, ln_g[i, 0], ln_b[i, 0])
        ffn = hier_moe(h, w_router_group[i], b_router_group[i], w_router_expert[i],
                       b_router_expert[i], w_gate[i], w_up[i], w_down[i])
        h = layer_norm(ALPHA * h + ffn, ln_g[i, 1], ln_b[i, 1])
        ple = (p[i] @ w_ple[i]) * jax.nn.sigmoid(h @ w_ple_gate[i])
        h = layer_norm(ALPHA * h + ple, ln_g[i, 2], ln_b[i, 2])
    return h


_drawn_inputs = setup_inputs


def setup_inputs(seed=0):
    import zlib

    import numpy as np

    out = dict(_drawn_inputs(seed))
    spreads = {}
    factors = {'b_router_group': 7.02, 'b_router_expert': 6.751}
    for name, (base, spread) in spreads.items():
        noise = np.random.default_rng([zlib.crc32(name.encode()), seed]).standard_normal(out[name].shape)
        drawn = base * np.exp(spread * noise) if base else spread * noise
        out[name] = jnp.asarray(drawn.astype(out[name].dtype))
    for name, factor in factors.items():
        out[name] = (out[name] * factor).astype(out[name].dtype)
    return out
```

```python
from contextlib import ExitStack

import concourse.bass as bass
from concourse import mybir

ALU = mybir.AluOpType
ACT = mybir.ActivationFunctionType
F32 = mybir.dt.float32
I32 = mybir.dt.int32
AX_X = mybir.AxisListType.X

P = 128
T = 256
TB = T // P
D = 1024
KC = D // P
DEPTH = 2
HEADS, KV_HEADS, HD = 8, 2, 128
GROUP = HEADS // KV_HEADS
KV = KV_HEADS * HD
IDX_HEADS, IDX_DIM = 4, 64
TOPK = min(256, T // 4)
NG, EPG = 4, 8
NE = NG * EPG
F = 512
PLE = 256
PC = PLE // P
ALPHA = (2.0 * DEPTH) ** 0.25
EPS = 1e-5
SCALE = HD ** -0.5
NEG = -1e30
TAKEN = -3e38

AW = P + T
BLK = (slice(0, P), slice(P, AW))

LANES = 4
CAP = P // LANES
ROUNDS = -(-T // CAP)
NGRP = NE // LANES
GATE_CHUNKS = D // (2 * P)
DOWN_CHUNKS = F // P
GCH = 2 * GATE_CHUNKS + DOWN_CHUNKS
SCRATCH = 7360
SLOTS = 8
SLOT = 4096
PAIR = 2 * GCH
assert PAIR % SLOTS == 0 and NGRP % 2 == 0

Q0, K0, V0 = 0, D, D + KV
IQ0 = D + 2 * KV
IK0 = IQ0 + IDX_HEADS * IDX_DIM
IW0 = IK0 + IDX_DIM
A_COLS = IW0 + IDX_HEADS
IDXW = A_COLS - IQ0


def trunk(nc, x, p, w_in_a, w_o_a, w_kv, w_q_b, w_o_b, w_rg, b_rg, w_re, b_re,
          w_gate, w_up, w_down, w_ple, w_pg, ln_g, ln_b, out):
    with ExitStack() as ctx:
        def sb(name, shape, dt=F32):
            return ctx.enter_context(nc.sbuf_tensor(name, shape, dt))

        def sem(name):
            return ctx.enter_context(nc.semaphore(name))

        bank = [ctx.enter_context(nc.psum_tensor(f"bank{i}", [P, 512], F32)) for i in range(8)]

        ring = sb("ring", [P, SLOTS, SLOT])
        h = sb("h", [P, TB, D])
        acc = sb("acc", [P, TB, D])
        hT = sb("hT", [P, KC, T])
        lnp = sb("lnp", [P, 2, D])
        lnrow = sb("lnrow", [1, D])
        scratch = sb("scratch", [P, SCRATCH])
        pT = sb("pT", [P, DEPTH, PC, T])
        wr = sb("wr", [P, DEPTH, KC, NG + NE])
        brow = sb("brow", [1, DEPTH, NG + NE])
        br = sb("br", [P, DEPTH, NG + NE])
        ident = sb("ident", [P, P])
        tri = sb("tri", [P, P])
        ones = sb("ones", [P, P])
        dist = sb("dist", [P, AW])
        causal = sb("causal", [P, AW])
        iota = sb("iota", [P, CAP])
        rev = sb("rev", [P, NE])
        small = sb("small", [P, 64])
        stats = sb("stats", [P, TB, 2, 6])
        mv = sb("mv", [P, TB, 5])
        lg = sb("lg", [P, TB, NG + NE])
        gsel = sb("gsel", [P, TB, NG])
        gtmp = sb("gtmp", [P, TB, NG])
        em = sb("em", [P, TB, NE])
        etmp = sb("etmp", [P, TB, NE])
        first = sb("first", [P, TB, NE])
        second = sb("second", [P, TB, NE])
        assign = sb("assign", [P, TB, NE])
        weight = sb("weight", [P, TB, NE])
        rank = sb("rank", [P, TB, NE])
        most = sb("most", [P, 1], I32)

        at = [0]

        def view(n):
            at[0] += n
            assert at[0] <= SCRATCH
            return scratch[:, at[0] - n:at[0]]

        qT = view(HEADS * T).rearrange("p (h t) -> p h t", h=HEADS)
        kT = view(KV_HEADS * T).rearrange("p (h t) -> p h t", h=KV_HEADS)
        v = view(TB * KV).rearrange("p (b c) -> p b c", b=TB)
        iqT = view(2 * T).rearrange("p (h t) -> p h t", h=2)
        ikT = view(T)
        iw = view(TB * IDX_HEADS).rearrange("p (b h) -> p b h", b=TB)
        score = view(AW)
        pen = view(AW)
        bias = view(2 * AW).rearrange("p (n c) -> p n c", n=2)
        prob = view(3 * AW).rearrange("p (n c) -> p n c", n=3)
        probT = view(2 * AW).rearrange("p (n c) -> p n c", n=2)
        top8 = view(8)
        at[0] -= 7 * AW + 8
        relu = view(4 * AW).rearrange("p (n c) -> p n c", n=4)
        at[0] = 0
        xgT = view(KC * P).rearrange("p (k s) -> p k s", k=KC)
        pick = view(TB * P).rearrange("p (b e s) -> p b e s", b=TB, e=LANES)
        wpick = view(TB * P).rearrange("p (b e s) -> p b e s", b=TB, e=LANES)
        pickT = view(T)
        sig = view(F)
        half = view(F)
        mid = view(F)
        midT = view(F).rearrange("p (c s) -> p c s", c=DOWN_CHUNKS)
        y = view(D)
        at[0] = 0
        gate = view(4 * 512).rearrange("p (n c) -> p n c", n=4)
        gated = view(4 * 512).rearrange("p (n c) -> p n c", n=4)
        at[0] = 0
        psb = view(DEPTH * TB * PLE).rearrange("p (l b c) -> p l b c", l=DEPTH, b=TB)

        x_in, small_in, p_in = sem("x_in"), sem("small_in"), sem("p_in")
        row_in, lnp_ready = sem("row_in"), sem("lnp_ready")
        vs = sem("vector_step")
        consts_ready = sem("consts_ready")
        bias_dot = sem("bias_dot")
        dense_landed = [sem(f"dense_landed{i}") for i in range(SLOTS)]
        dense_used = sem("dense_used")
        h_ready, turned = sem("h_ready"), sem("turned")
        hT_a, hT_v = sem("hT_by_scalar"), sem("hT_by_vector")
        p_turned, pT_ready = sem("p_turned"), sem("pT_ready")
        ln_stats, ln_scaled = sem("ln_stats"), sem("ln_scaled")
        routed, router_dot, ranked = sem("routed"), sem("router_dot"), sem("ranked")
        r_exp_in, r_exp = sem("router_exp_in"), sem("router_exp")
        max_ready = sem("max_ready")
        ple_dot, gate_dot, gate_sig = sem("ple_dot"), sem("gate_dot"), sem("gate_sig")
        mix_dot, out_sent = sem("mix_dot"), sem("out_sent")

        class Attention:

            def __init__(self, layer):
                self.idx_copied = sem(f"idx_copied_{layer}")
                self.k_dot = sem(f"k_dot_{layer}")
                self.kv_copied = sem(f"kv_copied_{layer}")
                self.q_copied = sem(f"q_copied_{layer}")
                self.rel_dot = sem(f"rel_dot_{layer}")
                self.relued = sem(f"relued_{layer}")
                self.qk = sem(f"qk_{layer}")
                self.logits = sem(f"logits_{layer}")
                self.peak = sem(f"peak_{layer}")
                self.exps = sem(f"exps_{layer}")
                self.normed = sem(f"normed_{layer}")
                self.p_turn = sem(f"p_turn_{layer}")
                self.probT_ready = sem(f"probT_ready_{layer}")
                self.pv = sem(f"pv_{layer}")
                self.o_copied = sem(f"o_copied_{layer}")

        class Pass:

            def __init__(self, name, credit):
                self.credit = credit
                self.landed = [sem(f"landed{i}_{name}") for i in range(SLOTS)]
                self.used = sem(f"used_{name}")
                self.picked = sem(f"picked_{name}")
                self.gathered = sem(f"gathered_{name}")
                self.xg = sem(f"xg_{name}")
                self.sigmoid = sem(f"sigmoid_{name}")
                self.mid = sem(f"mid_{name}")
                self.wturn = sem(f"wturn_{name}")
                self.pickT = sem(f"pickT_{name}")
                self.mturn = sem(f"mturn_{name}")
                self.midT = sem(f"midT_{name}")
                self.y = sem(f"y_{name}")
                self.comb = sem(f"comb_{name}")
                self.added = sem(f"added_{name}")

        attn = [Attention(layer) for layer in range(DEPTH)]
        main = [Pass(f"main{layer}", 0) for layer in range(DEPTH)]
        more = [Pass(f"more{layer}", SLOTS) for layer in range(DEPTH)]
        shifted = [sem(f"shifted{layer}") for layer in range(DEPTH)]

        def cols(w, c0, n):
            return w[:, c0:c0 + n].rearrange("(k p) n -> p k n", p=P), KC, n

        dense = [cols(w_in_a[0], IQ0, IDXW), cols(w_in_a[0], K0, 2 * KV), cols(w_in_a[0], Q0, 512),
                 cols(w_in_a[0], Q0 + 512, 512), cols(w_o_a[0], 0, 512), cols(w_o_a[0], 512, 512),
                 (w_ple[0].rearrange("(k p) n -> p k n", p=P), PC, D), cols(w_pg[0], 0, 512),
                 cols(w_pg[0], 512, 512), cols(w_kv, 0, 2 * KV), cols(w_q_b[0], 0, 512),
                 cols(w_q_b[0], 512, 512), cols(w_o_b[0], 0, 512), cols(w_o_b[0], 512, 512),
                 (w_ple[1].rearrange("(k p) n -> p k n", p=P), PC, D), cols(w_pg[1], 0, 512),
                 cols(w_pg[1], 512, 512)]
        A_IDX = 0
        W_KV, W_Q, W_O, W_PLE = (1, 9), (2, 10), (4, 12), (6, 14)
        BEFORE = (6, 14, len(dense))
        TURN = BEFORE[0] % SLOTS
        assert all(n % SLOTS == TURN for n in BEFORE[:DEPTH]) and len(dense) - BEFORE[1] <= SLOTS

        def dense_slot(j):
            return ring[:, j % SLOTS, 0:dense[j][1] * dense[j][2]].rearrange("p (k n) -> p k n", n=dense[j][2])

        def dense_here(eng, j):
            eng.wait_ge(dense_landed[j % SLOTS], 16 * (j // SLOTS + 1))

        def expert_slot(c):
            s = ring[:, (TURN + c) % SLOTS, :]
            if c % GCH < 2 * GATE_CHUNKS:
                return s.rearrange("p (e r f) -> p e r f", e=LANES, r=2)
            return s.rearrange("p (e n) -> p e n", e=LANES)

        def expert_here(eng, S, turn, c):
            eng.wait_ge(S.landed[(TURN + c) % SLOTS], turn * (16 * (PAIR // SLOTS)) + 16 * (c // SLOTS + 1))

        def gate_done(eng, S, n):
            eng.wait_ge(S.used, n * GCH + S.credit + GATE_CHUNKS)

        def up_done(eng, S, n):
            eng.wait_ge(S.used, n * GCH + S.credit + 2 * GATE_CHUNKS)

        def down_done(eng, S, n):
            eng.wait_ge(S.used, n * GCH + S.credit + GCH)

        def passes(eng, layer, group, new_round=None):
            S, M = main[layer], more[layer]
            with eng.Fori(0, NGRP // 2) as i:
                for q in range(2):
                    group(S, i * 2 + q, i * 2 + q, i, q)
            eng.wait_ge(S.added, 1 + 4 * NGRP)
            top = eng.value_load(most[0:1, 0:1], min_val=0, max_val=T)
            with eng.If(top > CAP):
                if new_round:
                    eng.sem_inc(M.added, 1)
                with eng.Fori(0, ROUNDS - 1) as r:
                    if new_round:
                        new_round(shifted[layer])
                    with eng.Fori(0, NGRP // 2) as i:
                        for q in range(2):
                            group(M, r * NGRP + i * 2 + q, i * 2 + q, r * (NGRP // 2) + i, q, (shifted[layer], r))
                eng.wait_ge(M.added, 1 + 4 * NGRP * (ROUNDS - 1))

        block = ctx.enter_context(nc.Block())

        @block.sync
        def _(sp):
            def load_dense(j):
                sp.dma_start(dense_slot(j), dense[j][0]).then_inc(dense_landed[j % SLOTS], 16)

            def load_expert(S, layer, first_group, c):
                j = c % GCH
                e0 = (first_group + c // GCH) * LANES
                if j < 2 * GATE_CHUNKS:
                    w = w_gate if j < GATE_CHUNKS else w_up
                    r0 = (j % GATE_CHUNKS) * 2 * P
                    src = w[layer, bass.ds(e0, LANES), r0:r0 + 2 * P, :].rearrange("e (p r) f -> p e (r f)", r=2)
                else:
                    r0 = (j - 2 * GATE_CHUNKS) * P
                    src = w_down[layer, bass.ds(e0, LANES), r0:r0 + P, :].rearrange("e p n -> p e n")
                dst = ring[:, (TURN + c) % SLOTS, :].rearrange("p (e n) -> p e n", e=LANES)
                sp.dma_start(dst, src).then_inc(S.landed[(TURN + c) % SLOTS], 16)

            for j in range(BEFORE[0]):
                load_dense(j)
            for layer in range(DEPTH):
                S, M = main[layer], more[layer]
                for c in range(SLOTS):
                    j = BEFORE[layer] + c - SLOTS
                    if j >= 0:
                        sp.wait_ge(dense_used, j + 1)
                    load_expert(S, layer, 0, c)
                with sp.Fori(0, NGRP // 2 - 1) as i:
                    for c in range(SLOTS, SLOTS + PAIR):
                        sp.wait_ge(S.used, i * PAIR + (c - SLOTS + 1))
                        load_expert(S, layer, i * 2, c)
                for c in range(SLOTS, PAIR):
                    sp.wait_ge(S.used, (NGRP // 2 - 1) * PAIR + c - SLOTS + 1)
                    load_expert(S, layer, NGRP - 2, c)
                sp.wait_ge(max_ready, layer + 1)
                top = sp.value_load(most[0:1, 0:1], min_val=0, max_val=T)
                with sp.If(top > CAP):
                    sp.wait_ge(S.used, NGRP * GCH)
                    sp.sem_inc(M.used, SLOTS)
                    with sp.Fori(0, ROUNDS - 1) as r:
                        with sp.Fori(0, NGRP // 2) as i:
                            for c in range(PAIR):
                                sp.wait_ge(M.used, r * (NGRP * GCH) + i * PAIR + (c + 1))
                                load_expert(M, layer, i * 2, c)
                    sp.wait_ge(M.used, SLOTS + (ROUNDS - 1) * NGRP * GCH)
                for j in range(BEFORE[layer], BEFORE[layer + 1]):
                    sp.wait_ge(S.used, NGRP * GCH - SLOTS + j - BEFORE[layer] + 1)
                    load_dense(j)
            sp.wait_ge(out_sent, 16 * TB)

        @block.gpsimd
        def _(pool):
            nc.gpsimd.iota(dist[:, BLK[0]], [[1, P]], base=0, channel_multiplier=-1,
                           allow_small_or_imprecise_dtypes=True).then_inc(consts_ready, 1)
            nc.gpsimd.iota(dist[:, BLK[1]], [[1, T]], base=-P, channel_multiplier=-1,
                           allow_small_or_imprecise_dtypes=True).then_inc(consts_ready, 1)
            nc.gpsimd.iota(iota[:, :], [[1, CAP]], base=0, channel_multiplier=0,
                           allow_small_or_imprecise_dtypes=True).then_inc(consts_ready, 1)
            nc.gpsimd.iota(rev[:, :], [[-1, NE]], base=NE, channel_multiplier=0,
                           allow_small_or_imprecise_dtypes=True).then_inc(consts_ready, 1)
            nc.gpsimd.memset(ones[:, :], 1.0).then_inc(consts_ready, 1)
            for n in range(3 * DEPTH):
                for k, par in enumerate((ln_g, ln_b)):
                    rows = 2 * n + k
                    if rows:
                        pool.wait_ge(lnp_ready, rows)
                    pool.dma_start(lnrow[0:1, :], par[n // 3, n % 3:n % 3 + 1, :]).then_inc(row_in, 16)
                    pool.wait_ge(row_in, 16 * (rows + 1))
                    if n and k == 0:
                        pool.wait_ge(h_ready, TB * n)
                    nc.gpsimd.partition_broadcast(lnp[:, k, :], lnrow[0:1, :]).then_inc(lnp_ready, 1)

        @block.scalar
        def _(act):
            for b in range(TB):
                act.dma_start(h[:, b, :], x[0, b * P:(b + 1) * P, :]).then_inc(x_in, 16)
            for layer in range(DEPTH):
                act.dma_start(psb[:, layer, :, :], p[layer, 0, :, :].rearrange("(b p) c -> p b c", p=P)).then_inc(p_in, 16)
                act.dma_start(wr[:, layer, :, 0:NG], w_rg[layer].rearrange("(k p) n -> p k n", p=P)).then_inc(small_in, 16)
                act.dma_start(wr[:, layer, :, NG:], w_re[layer].rearrange("(k p) n -> p k n", p=P)).then_inc(small_in, 16)
            act.dma_start(brow[0:1, :, 0:NG], b_rg.rearrange("(a l) n -> a l n", a=1)).then_inc(small_in, 16)
            act.dma_start(brow[0:1, :, NG:], b_re.rearrange("(a l) n -> a l n", a=1)).then_inc(small_in, 16)

            def copy_hT(event, first_bank):
                for b in range(TB):
                    act.wait_ge(turned, 4 * event + 2 * b + 1)
                    nc.scalar.copy(hT[:, 0:4, b * P:(b + 1) * P],
                                   bank[first_bank + 2 * b][:, :].rearrange("p (k t) -> p k t", k=4)).then_inc(hT_a, 1)

            def attention(layer, A):
                if layer == 0:
                    act.wait_ge(dense_used, A_IDX + 1)
                    nc.scalar.copy(iqT, bank[4][:, :].rearrange("p (h t) -> p h t", h=2)).then_inc(A.idx_copied, 1)
                    nc.scalar.copy(ikT, bank[5][:, 0:T]).then_inc(A.idx_copied, 1)
                    nc.scalar.mul(iw, bank[5][:, T:T + TB * IDX_HEADS].rearrange("p (b h) -> p b h", b=TB),
                                  IDX_HEADS ** -0.5).then_inc(A.idx_copied, 1)
                    for n in range(IDX_HEADS):
                        act.wait_ge(A.rel_dot, n + 1)
                        nc.scalar.activation(relu[:, n, :], bank[4 + n][:, 0:AW], ACT.Relu,
                                             scale=IDX_DIM ** -0.5).then_inc(A.relued, 1)
                kb = 4 if layer == 0 else 6
                act.wait_ge(A.k_dot, 1)
                nc.scalar.copy(kT, bank[kb][:, :].rearrange("p (h t) -> p h t", h=2)).then_inc(A.kv_copied, 1)
                act.wait_ge(dense_used, W_KV[layer] + 1)
                nc.scalar.copy(v, bank[kb + 1][:, :].rearrange("p (b c) -> p b c", b=TB)).then_inc(A.kv_copied, 1)
                for n in range(HEADS // 2):
                    act.wait_ge(dense_used, W_Q[layer] + n // 2 + 1)
                    nc.scalar.copy(qT[:, 2 * n:2 * n + 2, :],
                                   bank[n][:, :].rearrange("p (h t) -> p h t", h=2)).then_inc(A.q_copied, 1)

                def exps(n):
                    act.wait_ge(A.peak, 2 * n + 2)
                    for b in range(TB):
                        nc.scalar.activation(prob[:, n % 3, BLK[b]], prob[:, n % 3, BLK[b]], ACT.Exp,
                                             bias=small[:, 2 * n + b:2 * n + b + 1],
                                             accum_out=small[:, 16 + 2 * n + b:17 + 2 * n + b]).then_inc(A.exps, 1)

                def copies(n):
                    act.wait_ge(A.p_turn, n + 1)
                    if n >= 2:
                        act.wait_ge(A.pv, n - 1)
                    nc.scalar.copy(probT[:, n % 2, :], bank[4 + n % 2][:, 0:AW]).then_inc(A.probT_ready, 1)

                def outs(n):
                    act.wait_ge(A.pv, n + 1)
                    nc.scalar.copy(hT[:, n, :], bank[6 + n % 2][:, 0:T]).then_inc(A.o_copied, 1)

                for n in range(HEADS + 2):
                    if n < HEADS:
                        exps(n)
                    if 1 <= n <= HEADS:
                        copies(n - 1)
                    if n >= 2:
                        outs(n - 2)

            def layer_norm(n):
                for b in range(TB):
                    act.wait_ge(ln_stats, TB * n + b + 1)
                    nc.scalar.activation(h[:, b, :], acc[:, b, :], ACT.Identity, bias=mv[:, b, 3:4],
                                         scale=mv[:, b, 2:3]).then_inc(ln_scaled, 1)

            def router(layer):
                act.wait_ge(r_exp_in, 2 * layer + 1)
                nc.scalar.activation(gtmp[:, :, :], gtmp[:, :, :], ACT.Exp).then_inc(r_exp, 1)
                act.wait_ge(r_exp_in, 2 * layer + 2)
                nc.scalar.activation(small[:, 40:42], small[:, 40:42], ACT.Exp).then_inc(r_exp, 1)

            def expert_group(S, n, g, turn, q, round_=None):
                for k in range(2):
                    act.wait_ge(S.gathered, n * 2 + (k + 1))
                    nc.scalar.copy(xgT[:, 4 * k:4 * k + 4, :],
                                   bank[k][:, :].rearrange("p (k s) -> p k s", k=4)).then_inc(S.xg, 1)
                gate_done(act, S, n)
                nc.scalar.activation(sig, bank[2][:, :], ACT.Sigmoid).then_inc(S.sigmoid, 1)
                act.wait_ge(S.mturn, n + 1)
                nc.scalar.copy(midT, bank[6][:, :].rearrange("p (c s) -> p c s", c=DOWN_CHUNKS)).then_inc(S.midT, 1)
                down_done(act, S, n)
                for k in range(2):
                    nc.scalar.copy(y[:, k * 512:(k + 1) * 512], bank[4 + k][:, :]).then_inc(S.y, 1)

            act.wait_ge(p_turned, DEPTH)
            for layer in range(DEPTH):
                nc.scalar.copy(pT[:, layer, :, :], bank[6 + layer][:, :].rearrange("p (k t) -> p k t", k=PC)).then_inc(pT_ready, 1)
            copy_hT(0, 0)
            for layer in range(DEPTH):
                attention(layer, attn[layer])
                layer_norm(3 * layer)
                copy_hT(1 + 3 * layer, 0)
                router(layer)
                passes(act, layer, expert_group)
                layer_norm(3 * layer + 1)
                copy_hT(2 + 3 * layer, 4)
                for k in range(2):
                    for b in range(TB):
                        if b == 0:
                            act.wait_ge(gate_dot, 2 * layer + k + 1)
                        else:
                            act.wait_ge(dense_used, W_PLE[layer] + k + 2)
                        n = 2 * k + b
                        nc.scalar.activation(gate[:, n, :], bank[4 + n][:, :], ACT.Sigmoid).then_inc(gate_sig, 1)
                layer_norm(3 * layer + 2)
                if layer + 1 < DEPTH:
                    copy_hT(3 + 3 * layer, 0)
            for b in range(TB):
                act.wait_ge(h_ready, TB * 3 * DEPTH - TB + b + 1)
                act.dma_start(out[0, b * P:(b + 1) * P, :], h[:, b, :]).then_inc(out_sent, 16)

        @block.vector
        def _(dve):
            steps = [0]
            V = nc.vector

            def link(ins):
                steps[0] += 1
                ins.then_inc(vs, 1)
                dve.wait_ge(vs, steps[0])

            def copy_hT(event, first_bank):
                for b in range(TB):
                    dve.wait_ge(turned, 4 * event + 2 * b + 2)
                    V.tensor_copy(hT[:, 4:8, b * P:(b + 1) * P],
                                  bank[first_bank + 2 * b + 1][:, :].rearrange("p (k t) -> p k t", k=4)).then_inc(hT_v, 1)

            def sum_block(b):
                for k in range(2):
                    link(V.bn_stats(stats[:, b, k, :], acc[:, b, k * 512:(k + 1) * 512]))
                link(V.bn_aggr(mv[:, b, 0:2], stats[:, b, :, :]))
                var, dev, tmp = mv[:, b, 1:2], mv[:, b, 2:3], mv[:, b, 4:5]
                link(V.tensor_scalar(var, var, EPS, None, ALU.add))
                link(V.tensor_scalar(tmp.bitcast(I32), var.bitcast(I32), 1, None, ALU.logical_shift_right))
                link(V.tensor_scalar(dev.bitcast(I32), tmp.bitcast(I32), -1.0, float(0x5F3759DF), ALU.mult, ALU.add))
                for _ in range(3):
                    link(V.scalar_tensor_tensor(tmp, dev, var, dev, ALU.mult, ALU.mult))
                    link(V.tensor_scalar(tmp, tmp, -0.5, 1.5, ALU.mult, ALU.add))
                    link(V.tensor_tensor(dev, dev, tmp, ALU.mult))
                V.scalar_tensor_tensor(mv[:, b, 3:4], mv[:, b, 0:1], -1.0, mv[:, b, 2:3], ALU.mult, ALU.mult).then_inc(ln_stats, 1)

            def layer_norm(n):
                dve.wait_ge(lnp_ready, 2 * n + 2)
                for b in range(TB):
                    dve.wait_ge(ln_scaled, TB * n + b + 1)
                    link(V.tensor_tensor(h[:, b, :], h[:, b, :], lnp[:, 0, :], ALU.mult))
                    V.tensor_tensor(h[:, b, :], h[:, b, :], lnp[:, 1, :], ALU.add).then_inc(h_ready, 1)

            def pick_keys(A):
                dve.wait_ge(A.idx_copied, 3)
                for b in range(TB):
                    for n in range(IDX_HEADS):
                        if b == 0:
                            dve.wait_ge(A.relued, n + 1)
                        before = causal[:, BLK[b]] if n == 0 else score[:, BLK[b]]
                        link(V.scalar_tensor_tensor(score[:, BLK[b]], relu[:, n, BLK[b]], iw[:, b, n:n + 1],
                                                    before, ALU.mult, ALU.add))
                for b in range(TB):
                    for _ in range(TOPK // 8):
                        link(V.max(top8, score[:, BLK[b]]))
                        link(V.match_replace(score[:, BLK[b]], top8, score[:, BLK[b]], TAKEN))
                link(V.tensor_scalar(pen, score, TAKEN, NEG, ALU.is_gt, ALU.mult))
                link(V.tensor_tensor(pen, pen, causal[:, :], ALU.add))

            def attention(layer, A):
                if layer == 0:
                    pick_keys(A)
                mask = pen if layer == 0 else causal[:, :]

                def logits(n):
                    link(V.scalar_tensor_tensor(bias[:, n % 2, :], dist[:, :], 2.0 ** -(8 * (n + 1) / HEADS), mask,
                                                ALU.mult, ALU.add))
                    dve.wait_ge(A.qk, n + 1)
                    if n >= 3:
                        dve.wait_ge(A.p_turn, n - 2)
                    V.scalar_tensor_tensor(prob[:, n % 3, :], bank[n % 4][:, 0:AW], SCALE, bias[:, n % 2, :],
                                           ALU.mult, ALU.add).then_inc(A.logits, 1)
                    dve.wait_ge(A.logits, n + 1)
                    for b in range(TB):
                        V.tensor_reduce(small[:, 2 * n + b:2 * n + b + 1], prob[:, n % 3, BLK[b]], AX_X, ALU.max,
                                        negate=True).then_inc(A.peak, 1)

                def norms(n):
                    dve.wait_ge(A.exps, 2 * n + 2)
                    link(V.reciprocal(small[:, 32:34], small[:, 16 + 2 * n:18 + 2 * n]))
                    for b in range(TB):
                        V.tensor_scalar(prob[:, n % 3, BLK[b]], prob[:, n % 3, BLK[b]], small[:, 32 + b:33 + b], None,
                                        ALU.mult).then_inc(A.normed, 1)
                    dve.wait_ge(A.normed, 2 * n + 2)

                for n in range(HEADS + 1):
                    if n < HEADS:
                        logits(n)
                    if n:
                        norms(n - 1)
                for k in range(2):
                    for b in range(TB):
                        if b == 0:
                            dve.wait_ge(mix_dot, 2 * layer + k + 1)
                        else:
                            dve.wait_ge(dense_used, W_O[layer] + k + 1)
                        link(V.scalar_tensor_tensor(acc[:, b, k * 512:(k + 1) * 512], h[:, b, k * 512:(k + 1) * 512],
                                                    ALPHA, bank[2 * k + b][:, :], ALU.mult, ALU.add))
                        if k == 1:
                            sum_block(b)

            def wide(a, shape):
                return a.broadcast_to(shape)

            def router(layer):
                full = [P, TB, NE]
                dve.wait_ge(router_dot, layer + 1)
                link(V.tensor_tensor(lg[:, :, :], bank[4][:, 0:TB * (NG + NE)].rearrange("p (b n) -> p b n", b=TB),
                                     wide(br[:, layer:layer + 1, :], [P, TB, NG + NE]), ALU.add))
                g, e = lg[:, :, 0:NG], lg[:, :, NG:]

                def argmax(values, onehot, tmp, width, peak):
                    link(V.tensor_reduce(peak, values, AX_X, ALU.max))
                    each = [P, TB, width]
                    link(V.tensor_tensor(tmp, values, wide(peak.unsqueeze(2), each), ALU.is_equal))
                    link(V.tensor_tensor(tmp, tmp, wide(rev[:, 0:width].unsqueeze(1), each), ALU.mult))
                    link(V.tensor_reduce(small[:, 36:38], tmp, AX_X, ALU.max))
                    link(V.tensor_tensor(onehot, tmp, wide(small[:, 36:38].unsqueeze(2), each), ALU.is_equal))

                argmax(g, gsel[:, :, :], gtmp[:, :, :], NG, small[:, 34:36])
                V.tensor_tensor(gtmp[:, :, :], g, wide(small[:, 34:36].unsqueeze(2), [P, TB, NG]),
                                ALU.subtract).then_inc(r_exp_in, 1)
                four = [P, TB, NG, EPG]
                sel4 = wide(gsel[:, :, :].unsqueeze(3), four)
                em4 = em[:, :, :].rearrange("p b (g e) -> p b g e", g=NG)
                tmp4 = etmp[:, :, :].rearrange("p b (g e) -> p b g e", g=NG)
                link(V.tensor_tensor(em4, e.rearrange("p b (g e) -> p b g e", g=NG), sel4, ALU.mult))
                link(V.tensor_scalar(tmp4, sel4, -NEG, NEG, ALU.mult, ALU.add))
                link(V.tensor_tensor(em[:, :, :], em[:, :, :], etmp[:, :, :], ALU.add))
                argmax(em[:, :, :], first[:, :, :], etmp[:, :, :], NE, small[:, 38:40])
                link(V.scalar_tensor_tensor(em[:, :, :], first[:, :, :], TAKEN, em[:, :, :], ALU.mult, ALU.add))
                argmax(em[:, :, :], second[:, :, :], etmp[:, :, :], NE, small[:, 40:42])
                V.tensor_tensor(assign[:, :, :], first[:, :, :], second[:, :, :], ALU.add).then_inc(routed, 1)
                V.tensor_tensor(small[:, 40:42], small[:, 40:42], small[:, 38:40], ALU.subtract).then_inc(r_exp_in, 1)
                dve.wait_ge(r_exp, 2 * layer + 1)
                link(V.tensor_reduce(small[:, 42:44], gtmp[:, :, :], AX_X, ALU.add))
                dve.wait_ge(r_exp, 2 * layer + 2)
                link(V.tensor_scalar(small[:, 44:46], small[:, 40:42], 1.0, None, ALU.add))
                link(V.tensor_tensor(small[:, 42:44], small[:, 42:44], small[:, 44:46], ALU.mult))
                link(V.reciprocal(small[:, 46:48], small[:, 42:44]))
                link(V.tensor_tensor(small[:, 44:46], small[:, 46:48], small[:, 40:42], ALU.mult))
                link(V.tensor_tensor(weight[:, :, :], first[:, :, :], wide(small[:, 46:48].unsqueeze(2), full), ALU.mult))
                link(V.tensor_tensor(etmp[:, :, :], second[:, :, :], wide(small[:, 44:46].unsqueeze(2), full), ALU.mult))
                link(V.tensor_tensor(weight[:, :, :], weight[:, :, :], etmp[:, :, :], ALU.add))
                dve.wait_ge(ranked, layer + 1)
                dve.wait_ge(routed, layer + 1)
                link(V.scalar_tensor_tensor(rank[:, :, :], bank[5][:, 0:TB * NE].rearrange("p (b e) -> p b e", b=TB), 1.0,
                                            assign[:, :, :], ALU.add, ALU.mult))
                link(V.tensor_scalar(rank[:, :, :], rank[:, :, :], -1.0, None, ALU.add))
                V.tensor_reduce(most[:, :], bank[5][:, TB * NE:(TB + 1) * NE], AX_X, ALU.max).then_inc(max_ready, 1)
                V.tensor_scalar(acc[:, :, :], h[:, :, :], ALPHA, None, ALU.mult).then_inc(main[layer].added, 1)

            def expert_group(S, n, g, turn, q, round_=None):
                four = [P, TB, LANES, CAP]

                def mine(a):
                    return wide(a[:, :, bass.ds(g * LANES, LANES)].unsqueeze(3), four)

                if round_:
                    dve.wait_ge(round_[0], round_[1] + 1)
                V.tensor_tensor(pick, wide(iota[:, :].unsqueeze(1).unsqueeze(1), four), mine(rank), ALU.is_equal).then_inc(S.picked, 1)
                dve.wait_ge(S.picked, n * 2 + 1)
                V.tensor_tensor(wpick, pick, mine(weight), ALU.mult).then_inc(S.picked, 1)
                dve.wait_ge(S.sigmoid, n + 1)
                V.tensor_tensor(half, bank[2][:, :], sig, ALU.mult).then_inc(S.mid, 1)
                dve.wait_ge(S.mid, n * 2 + 1)
                up_done(dve, S, n)
                V.tensor_tensor(mid, half, bank[3][:, :], ALU.mult).then_inc(S.mid, 1)
                dve.wait_ge(S.wturn, n + 1)
                V.tensor_copy(pickT, bank[7][:, 0:T]).then_inc(S.pickT, 1)
                dve.wait_ge(S.added, n * 4 + 1)
                for k in range(4):
                    dve.wait_ge(S.comb, n * 4 + (k + 1))
                    a = acc[:, k // 2, (k % 2) * 512:(k % 2 + 1) * 512]
                    V.tensor_tensor(a, a, bank[k][:, :], ALU.add).then_inc(S.added, 1)

            def next_round(done):
                V.tensor_scalar(rank[:, :, :], rank[:, :, :], -float(CAP), None, ALU.add).then_inc(done, 1)

            dve.wait_ge(consts_ready, 5)
            link(V.tensor_scalar(ident[:, :], dist[:, BLK[0]], 0.0, None, ALU.is_equal))
            link(V.tensor_scalar(tri[:, :], dist[:, BLK[0]], 0.0, None, ALU.is_gt))
            V.tensor_scalar(causal[:, :], dist[:, :], 0.0, NEG, ALU.is_gt, ALU.mult).then_inc(consts_ready, 1)
            dve.wait_ge(consts_ready, 6)
            dve.wait_ge(bias_dot, 1)
            link(V.tensor_copy(br[:, :, :], bank[5][:, 0:DEPTH * (NG + NE)].rearrange("p (l n) -> p l n", l=DEPTH)))
            copy_hT(0, 0)
            for layer in range(DEPTH):
                attention(layer, attn[layer])
                layer_norm(3 * layer)
                copy_hT(1 + 3 * layer, 0)
                router(layer)
                passes(dve, layer, expert_group, next_round)
                for b in range(TB):
                    sum_block(b)
                layer_norm(3 * layer + 1)
                copy_hT(2 + 3 * layer, 4)
                for k in range(2):
                    for b in range(TB):
                        n = 2 * k + b
                        dve.wait_ge(gate_sig, 4 * layer + n + 1)
                        if n < 3:
                            dve.wait_ge(ple_dot, 3 * layer + n + 1)
                        else:
                            dve.wait_ge(dense_used, W_PLE[layer] + 1)
                        link(V.tensor_tensor(gated[:, n, :], bank[n][:, :], gate[:, n, :], ALU.mult))
                        dve.wait_ge(h_ready, TB * (3 * layer + 2))
                        link(V.scalar_tensor_tensor(acc[:, b, k * 512:(k + 1) * 512], h[:, b, k * 512:(k + 1) * 512],
                                                    ALPHA, gated[:, n, :], ALU.mult, ALU.add))
                        if k == 1:
                            sum_block(b)
                layer_norm(3 * layer + 2)
                if layer + 1 < DEPTH:
                    copy_hT(3 + 3 * layer, 0)

        @block.tensor
        def _(pe):
            mm, transpose = nc.tensor.matmul, nc.tensor.transpose

            def turn(event, first_bank):
                for b in range(TB):
                    if event == 0:
                        pe.wait_ge(x_in, 16 * TB)
                    else:
                        pe.wait_ge(h_ready, TB * (event - 1) + b + 1)
                    for k in range(KC):
                        ins = transpose(bank[first_bank + 2 * b + k // 4][:, (k % 4) * P:(k % 4 + 1) * P],
                                        h[:, b, k * P:(k + 1) * P], ident[:, :])
                        if k % 4 == 3:
                            ins.then_inc(turned, 1)
                pe.wait_ge(hT_a, TB * (event + 1))
                pe.wait_ge(hT_v, TB * (event + 1))

            def columns(o, w, c0, n):
                for k in range(KC):
                    ins = mm(o, w[:, k, c0:c0 + n], hT[:, k, :], start=(k == 0), stop=(k == KC - 1))
                return ins

            def rows(o, w, b, c0, n):
                for k in range(KC):
                    ins = mm(o, hT[:, k, b * P:(b + 1) * P], w[:, k, c0:c0 + n], start=(k == 0), stop=(k == KC - 1))
                return ins

            def index_scores(A):
                dense_here(pe, A_IDX)
                w = dense_slot(A_IDX)
                for n in range(2):
                    columns(bank[4][:, n * T:(n + 1) * T], w, n * P, P)
                for n in range(2):
                    columns(bank[5][n * IDX_DIM:(n + 1) * IDX_DIM, 0:T], w, IK0 - IQ0, IDX_DIM)
                for b in range(TB):
                    ins = rows(bank[5][:, T + b * IDX_HEADS:T + (b + 1) * IDX_HEADS], w, b, IW0 - IQ0, IDX_HEADS)
                ins.then_inc(dense_used, 1)
                pe.wait_ge(A.idx_copied, 3)
                for n in range(IDX_HEADS):
                    part = slice(IDX_DIM * (n % 2), IDX_DIM * (n % 2 + 1))
                    for b in range(TB):
                        ins = mm(bank[4 + n][:, BLK[b]], iqT[part, n // 2, b * P:(b + 1) * P],
                                 ikT[part, 0:P * (b + 1)], start=True, stop=True)
                    ins.then_inc(A.rel_dot, 1)
                pe.wait_ge(A.relued, 2)

            def attention(layer, A):
                if layer == 0:
                    index_scores(A)
                kb = 4 if layer == 0 else 6
                dense_here(pe, W_KV[layer])
                w = dense_slot(W_KV[layer])
                for n in range(KV_HEADS):
                    ins = columns(bank[kb][:, n * T:(n + 1) * T], w, n * P, P)
                ins.then_inc(A.k_dot, 1)
                for b in range(TB):
                    ins = rows(bank[kb + 1][:, b * KV:(b + 1) * KV], w, b, KV, KV)
                ins.then_inc(dense_used, 1)
                for n in range(HEADS):
                    j = W_Q[layer] + n // 4
                    if n % 4 == 0:
                        dense_here(pe, j)
                    ins = columns(bank[n // 2][:, (n % 2) * T:(n % 2 + 1) * T], dense_slot(j), (n % 4) * P, P)
                    if n % 4 == 3:
                        ins.then_inc(dense_used, 1)
                pe.wait_ge(A.kv_copied, 2)
                pe.wait_ge(A.q_copied, HEADS // 2)

                def qk(n):
                    if n >= 4:
                        pe.wait_ge(A.logits, n - 3)
                    for b in range(TB):
                        ins = mm(bank[n % 4][:, BLK[b]], qT[:, n, b * P:(b + 1) * P],
                                 kT[:, n // GROUP, 0:P * (b + 1)], start=True, stop=True)
                    ins.then_inc(A.qk, 1)

                def turn_prob(n):
                    pe.wait_ge(A.normed, 2 * n + 2)
                    if n >= 2:
                        pe.wait_ge(A.probT_ready, n - 1)
                    for k in range(3):
                        ins = transpose(bank[4 + n % 2][:, k * P:(k + 1) * P], prob[:, n % 3, k * P:(k + 1) * P], ident[:, :])
                    ins.then_inc(A.p_turn, 1)

                def pv(n):
                    pe.wait_ge(A.probT_ready, n + 1)
                    if n >= 2:
                        pe.wait_ge(A.o_copied, n - 1)
                    o, hd = bank[6 + n % 2], slice(n // GROUP * HD, (n // GROUP + 1) * HD)
                    mm(o[:, 0:T], v[:, 0, hd], probT[:, n % 2, 0:T], start=True, stop=False)
                    mm(o[:, P:T], v[:, 1, hd], probT[:, n % 2, T:AW], start=False, stop=True).then_inc(A.pv, 1)

                for n in range(3):
                    qk(n)
                for n in range(HEADS + 1):
                    if n < HEADS:
                        turn_prob(n)
                    if n + 3 < HEADS:
                        qk(n + 3)
                    if n:
                        pv(n - 1)
                pe.wait_ge(A.o_copied, HEADS)
                for k in range(2):
                    j = W_O[layer] + k
                    dense_here(pe, j)
                    for b in range(TB):
                        rows(bank[2 * k + b][:, :], dense_slot(j), b, 0, 512).then_inc((mix_dot, dense_used)[b], 1)

            def router(layer):
                for b in range(TB):
                    for k in range(KC):
                        ins = mm(bank[4][:, b * (NG + NE):(b + 1) * (NG + NE)], hT[:, k, b * P:(b + 1) * P],
                                 wr[:, layer, k, :], start=(k == 0), stop=(k == KC - 1))
                ins.then_inc(router_dot, 1)
                pe.wait_ge(routed, layer + 1)
                mm(bank[5][:, 0:NE], tri[:, :], assign[:, 0, :], start=True, stop=True)
                mm(bank[5][:, NE:2 * NE], ones[:, :], assign[:, 0, :], start=True, stop=False)
                mm(bank[5][:, NE:2 * NE], tri[:, :], assign[:, 1, :], start=False, stop=True)
                for b in range(TB):
                    ins = mm(bank[5][:, 2 * NE:3 * NE], ones[:, :], assign[:, b, :], start=(b == 0), stop=(b == 1))
                ins.then_inc(ranked, 1)

            def expert_group(S, n, g, turn, q, round_=None):
                pe.wait_ge(S.picked, n * 2 + 1)
                pe.wait_ge(S.added, n * 4 + 1)
                for k in range(KC):
                    r0 = k // 2 * 2 * P
                    r = h[:, :, r0:r0 + 2 * P].rearrange("p b (d r) -> p b r d", r=2)
                    for b in range(TB):
                        ins = mm(bank[k // 4][:, (k % 4) * P:(k % 4 + 1) * P], r[:, b, k % 2, :],
                                 pick[:, b].rearrange("p e s -> p (e s)"), start=(b == 0), stop=(b == 1))
                    if k % 4 == 3:
                        ins.then_inc(S.gathered, 1)
                pe.wait_ge(S.picked, n * 2 + 2)
                for b in range(TB):
                    ins = transpose(bank[7][:, b * P:(b + 1) * P], wpick[:, b].rearrange("p e s -> p (e s)"), ident[:, :])
                ins.then_inc(S.wturn, 1)
                pe.wait_ge(S.xg, n * 2 + 2)
                c = q * GCH
                for o in (bank[2], bank[3]):
                    for k in range(KC):
                        if k % 2 == 0:
                            expert_here(pe, S, turn, c)
                        for e in range(LANES):
                            lane = slice(e * CAP, (e + 1) * CAP)
                            ins = mm(o[lane, :], xgT[:, k, lane], expert_slot(c)[:, e, k % 2, :],
                                     start=(k == 0), stop=(k == KC - 1))
                        if k % 2:
                            ins.then_inc(S.used, 1)
                            c += 1
                pe.wait_ge(S.mid, n * 2 + 2)
                for k in range(DOWN_CHUNKS):
                    ins = transpose(bank[6][:, k * P:(k + 1) * P], mid[:, k * P:(k + 1) * P], ident[:, :])
                ins.then_inc(S.mturn, 1)
                pe.wait_ge(S.midT, n + 1)
                for k in range(DOWN_CHUNKS):
                    expert_here(pe, S, turn, c)
                    for half_ in range(2):
                        for e in range(LANES):
                            lane = slice(e * CAP, (e + 1) * CAP)
                            ins = mm(bank[4 + half_][lane, :], midT[:, k, lane],
                                     expert_slot(c)[:, e, half_ * 512:(half_ + 1) * 512],
                                     start=(k == 0), stop=(k == DOWN_CHUNKS - 1))
                    ins.then_inc(S.used, 1)
                    c += 1
                pe.wait_ge(S.pickT, n + 1)
                pe.wait_ge(S.y, n * 2 + 2)
                for k in range(4):
                    b, half_ = k // 2, k % 2
                    mm(bank[k][:, :], pickT[:, b * P:(b + 1) * P], y[:, half_ * 512:(half_ + 1) * 512],
                       start=True, stop=True).then_inc(S.comb, 1)

            pe.wait_ge(consts_ready, 6)
            pe.wait_ge(small_in, 16 * (2 * DEPTH + 2))
            mm(bank[5][:, 0:DEPTH * (NG + NE)], ones[0:1, :], brow[0:1, :, :].rearrange("p l n -> p (l n)"),
               start=True, stop=True).then_inc(bias_dot, 1)
            pe.wait_ge(p_in, 16 * DEPTH)
            for layer in range(DEPTH):
                for k in range(PC):
                    for b in range(TB):
                        ins = transpose(bank[6 + layer][:, k * T + b * P:k * T + (b + 1) * P],
                                        psb[:, layer, b, k * P:(k + 1) * P], ident[:, :])
                ins.then_inc(p_turned, 1)
            pe.wait_ge(pT_ready, DEPTH)
            turn(0, 0)
            for layer in range(DEPTH):
                attention(layer, attn[layer])
                turn(1 + 3 * layer, 0)
                router(layer)
                passes(pe, layer, expert_group)
                dense_here(pe, W_PLE[layer])
                for k in range(2):
                    for b in range(TB):
                        for c in range(PC):
                            ins = mm(bank[2 * k + b][:, :], pT[:, layer, c, b * P:(b + 1) * P],
                                     dense_slot(W_PLE[layer])[:, c, k * 512:(k + 1) * 512], start=(c == 0), stop=(c == PC - 1))
                        if k * TB + b < 3:
                            ins.then_inc(ple_dot, 1)
                        else:
                            ins.then_inc(dense_used, 1)
                turn(2 + 3 * layer, 4)
                for k in range(2):
                    j = W_PLE[layer] + 1 + k
                    dense_here(pe, j)
                    for b in range(TB):
                        rows(bank[4 + 2 * k + b][:, :], dense_slot(j), b, 0, 512).then_inc((gate_dot, dense_used)[b], 1)
                if layer + 1 < DEPTH:
                    turn(3 + 3 * layer, 0)


INPUTS = ["x", "p", "w_in_a", "w_o_a", "w_kv_shared", "w_q_b", "w_o_b", "w_router_group", "b_router_group",
          "w_router_expert", "b_router_expert", "w_gate", "w_up", "w_down", "w_ple", "w_ple_gate", "ln_g", "ln_b"]


def kernel(**inputs):
    import numpy as np
    import concourse.bacc as bacc
    from concourse.bass_utils import run_bass_kernel_spmd

    nc = bacc.Bacc("TRN2", target_bir_lowering=False, num_devices=1)
    arrays, args = {}, []
    for name in INPUTS:
        a = np.ascontiguousarray(inputs[name])
        arrays[f"in_{name}"] = a
        args.append(nc.dram_tensor(f"in_{name}", a.shape, mybir.dt.from_np(a.dtype), kind="ExternalInput").ap())
    args.append(nc.dram_tensor("out_h", (1, T, D), F32, kind="ExternalOutput").ap())
    trunk(nc, *args)
    r = run_bass_kernel_spmd(nc, [arrays], core_ids=[0])
    return r.results[0]["out_h"]
```

```python
from contextlib import ExitStack

import concourse.bass as bass
from concourse import mybir

ALU = mybir.AluOpType
ACT = mybir.ActivationFunctionType
F32 = mybir.dt.float32
I32 = mybir.dt.int32
AX_X = mybir.AxisListType.X

P = 128
T = 256
TB = T // P
D = 1024
KC = D // P
DEPTH = 2
HEADS, KV_HEADS, HD = 8, 2, 128
GROUP = HEADS // KV_HEADS
KV = KV_HEADS * HD
IDX_HEADS, IDX_DIM = 4, 64
TOPK = min(256, T // 4)
NG, EPG = 4, 8
NE = NG * EPG
F = 512
PLE = 256
PC = PLE // P
ALPHA = (2.0 * DEPTH) ** 0.25
EPS = 1e-5
SCALE = HD ** -0.5
NEG = -1e30
TAKEN = -3e38

AW = P + T
BLK = (slice(0, P), slice(P, AW))

LANES = 4
CAP = P // LANES
ROUNDS = -(-T // CAP)
NGRP = NE // LANES
GATE_CHUNKS = D // (2 * P)
DOWN_CHUNKS = F // P
GCH = 2 * GATE_CHUNKS + DOWN_CHUNKS
SCRATCH = 7360
SLOTS = 8
SLOT = 4096
PAIR = 2 * GCH
assert PAIR % SLOTS == 0 and NGRP % 2 == 0

Q0, K0, V0 = 0, D, D + KV
IQ0 = D + 2 * KV
IK0 = IQ0 + IDX_HEADS * IDX_DIM
IW0 = IK0 + IDX_DIM
A_COLS = IW0 + IDX_HEADS
IDXW = A_COLS - IQ0


def trunk(nc, x, p, w_in_a, w_o_a, w_kv, w_q_b, w_o_b, w_router, b_router,
          w_gate, w_up, w_down, w_ple, w_pg, ln_g, ln_b, out):
    with ExitStack() as ctx:
        def sb(name, shape, dt=F32):
            return ctx.enter_context(nc.sbuf_tensor(name, shape, dt))

        def sem(name):
            return ctx.enter_context(nc.semaphore(name))

        bank = [ctx.enter_context(nc.psum_tensor(f"bank{i}", [P, 512], F32)) for i in range(8)]

        ring = sb("ring", [P, SLOTS, SLOT])
        h = sb("h", [P, TB, D])
        acc = sb("acc", [P, TB, D])
        hT = sb("hT", [P, KC, T])
        lnp = sb("lnp", [P, 2, D])
        lnrow = sb("lnrow", [1, D])
        scratch = sb("scratch", [P, SCRATCH])
        pT = sb("pT", [P, DEPTH, PC, T])
        wr = sb("wr", [P, DEPTH, KC, NG + NE])
        brow = sb("brow", [1, DEPTH, NG + NE])
        ident = sb("ident", [P, P])
        tri = sb("tri", [P, P])
        ones = sb("ones", [P, P])
        dist = sb("dist", [P, AW])
        causal = sb("causal", [P, AW])
        iota = sb("iota", [P, CAP])
        rev = sb("rev", [P, NE])
        small = sb("small", [P, 64])
        stats = sb("stats", [P, TB, 2, 6])
        mv = sb("mv", [P, TB, 4])
        lg = sb("lg", [P, TB, NG + NE])
        gsel = sb("gsel", [P, TB, NG])
        gtmp = sb("gtmp", [P, TB, NG])
        em = sb("em", [P, TB, NE])
        etmp = sb("etmp", [P, TB, NE])
        first = sb("first", [P, TB, NE])
        second = sb("second", [P, TB, NE])
        assign = sb("assign", [P, TB, NE])
        weight = sb("weight", [P, TB, NE])
        rank = sb("rank", [P, TB, NE])
        most = sb("most", [P, 1], I32)

        at = [0]

        def view(n):
            at[0] += n
            assert at[0] <= SCRATCH
            return scratch[:, at[0] - n:at[0]]

        qT = view(HEADS * T).rearrange("p (h t) -> p h t", h=HEADS)
        kT = view(KV_HEADS * T).rearrange("p (h t) -> p h t", h=KV_HEADS)
        v = view(TB * KV).rearrange("p (b c) -> p b c", b=TB)
        iqT = view(2 * T).rearrange("p (h t) -> p h t", h=2)
        ikT = view(T)
        iw = view(TB * IDX_HEADS).rearrange("p (b h) -> p b h", b=TB)
        score = view(AW)
        pen = view(AW)
        bias = view(2 * AW).rearrange("p (n c) -> p n c", n=2)
        prob = view(2 * AW).rearrange("p (n c) -> p n c", n=2)
        probT = view(AW)
        top8 = view(8)
        at[0] -= 5 * AW + 8
        relu = view(4 * AW).rearrange("p (n c) -> p n c", n=4)
        at[0] = 0
        xgT = view(KC * P).rearrange("p (k s) -> p k s", k=KC)
        pick = view(TB * P).rearrange("p (b e s) -> p b e s", b=TB, e=LANES)
        wpick = view(TB * P).rearrange("p (b e s) -> p b e s", b=TB, e=LANES)
        pickT = view(T)
        sig = view(F)
        half = view(F)
        mid = view(F)
        midT = view(F).rearrange("p (c s) -> p c s", c=DOWN_CHUNKS)
        y = view(D)
        at[0] = 0
        gate = view(4 * 512).rearrange("p (n c) -> p n c", n=4)
        gated = view(4 * 512).rearrange("p (n c) -> p n c", n=4)
        at[0] = 0
        psb = view(DEPTH * TB * PLE).rearrange("p (l b c) -> p l b c", l=DEPTH, b=TB)

        x_in, small_in, p_in = sem("x_in"), sem("small_in"), sem("p_in")
        row_in, lnp_ready = sem("row_in"), sem("lnp_ready")
        vs = sem("vector_step")
        consts_ready = sem("consts_ready")
        dense_landed = [sem(f"dense_landed{i}") for i in range(SLOTS)]
        dense_used = sem("dense_used")
        h_ready, turned = sem("h_ready"), sem("turned")
        hT_ready = sem("hT_ready")
        p_turned, pT_ready = sem("p_turned"), sem("pT_ready")
        routed, router_dot, ranked = sem("routed"), sem("router_dot"), sem("ranked")
        r_exp_in, r_exp = sem("router_exp_in"), sem("router_exp")
        max_ready = sem("max_ready")
        ple_dot, gate_dot, gate_sig = sem("ple_dot"), sem("gate_dot"), sem("gate_sig")
        mix_dot, out_sent = sem("mix_dot"), sem("out_sent")

        class Attention:

            def __init__(self, layer):
                self.idx_copied = sem(f"idx_copied_{layer}")
                self.k_dot = sem(f"k_dot_{layer}")
                self.q_dot = sem(f"q_dot_{layer}")
                self.kv_copied = sem(f"kv_copied_{layer}")
                self.q_copied = sem(f"q_copied_{layer}")
                self.rel_dot = sem(f"rel_dot_{layer}")
                self.relued = sem(f"relued_{layer}")
                self.qk = sem(f"qk_{layer}")
                self.logits = sem(f"logits_{layer}")
                self.peak = sem(f"peak_{layer}")
                self.exps = sem(f"exps_{layer}")
                self.normed = sem(f"normed_{layer}")
                self.p_turn = sem(f"p_turn_{layer}")
                self.probT_ready = sem(f"probT_ready_{layer}")
                self.pv = sem(f"pv_{layer}")
                self.o_copied = sem(f"o_copied_{layer}")

        class Pass:

            def __init__(self, name, credit):
                self.credit = credit
                self.landed = [sem(f"landed{i}_{name}") for i in range(SLOTS)]
                self.used = sem(f"used_{name}")
                self.picked = sem(f"picked_{name}")
                self.gathered = sem(f"gathered_{name}")
                self.xg = sem(f"xg_{name}")
                self.sigmoid = sem(f"sigmoid_{name}")
                self.mid = sem(f"mid_{name}")
                self.wturn = sem(f"wturn_{name}")
                self.pickT = sem(f"pickT_{name}")
                self.mturn = sem(f"mturn_{name}")
                self.midT = sem(f"midT_{name}")
                self.y = sem(f"y_{name}")
                self.comb = sem(f"comb_{name}")
                self.added = sem(f"added_{name}")

        attn = [Attention(layer) for layer in range(DEPTH)]
        main = [Pass(f"main{layer}", 0) for layer in range(DEPTH)]
        more = [Pass(f"more{layer}", SLOTS) for layer in range(DEPTH)]
        shifted = [sem(f"shifted{layer}") for layer in range(DEPTH)]

        def cols(w, c0, n):
            return w[:, c0:c0 + n].rearrange("(k p) n -> p k n", p=P), KC, n

        dense = [cols(w_in_a[0], IQ0, IDXW), cols(w_in_a[0], K0, 2 * KV), cols(w_in_a[0], Q0, 512),
                 cols(w_in_a[0], Q0 + 512, 512), cols(w_o_a[0], 0, 512), cols(w_o_a[0], 512, 512),
                 (w_ple[0].rearrange("(k p) n -> p k n", p=P), PC, D), cols(w_pg[0], 0, 512),
                 cols(w_pg[0], 512, 512), cols(w_kv, 0, 2 * KV), cols(w_q_b[0], 0, 512),
                 cols(w_q_b[0], 512, 512), cols(w_o_b[0], 0, 512), cols(w_o_b[0], 512, 512),
                 (w_ple[1].rearrange("(k p) n -> p k n", p=P), PC, D), cols(w_pg[1], 0, 512),
                 cols(w_pg[1], 512, 512)]
        A_IDX = 0
        W_KV, W_Q, W_O, W_PLE = (1, 9), (2, 10), (4, 12), (6, 14)
        BEFORE = (6, 14, len(dense))
        TURN = BEFORE[0] % SLOTS
        assert all(n % SLOTS == TURN for n in BEFORE[:DEPTH]) and len(dense) - BEFORE[1] <= SLOTS

        def dense_slot(j):
            return ring[:, j % SLOTS, 0:dense[j][1] * dense[j][2]].rearrange("p (k n) -> p k n", n=dense[j][2])

        def dense_here(eng, j):
            eng.wait_ge(dense_landed[j % SLOTS], 16 * (j // SLOTS + 1))

        def expert_slot(c):
            s = ring[:, (TURN + c) % SLOTS, :]
            if c % GCH < 2 * GATE_CHUNKS:
                return s.rearrange("p (e r f) -> p e r f", e=LANES, r=2)
            return s.rearrange("p (e n) -> p e n", e=LANES)

        def expert_here(eng, S, turn, c):
            eng.wait_ge(S.landed[(TURN + c) % SLOTS], turn * (16 * (PAIR // SLOTS)) + 16 * (c // SLOTS + 1))

        def gate_done(eng, S, n):
            eng.wait_ge(S.used, n * GCH + S.credit + GATE_CHUNKS)

        def up_done(eng, S, n):
            eng.wait_ge(S.used, n * GCH + S.credit + 2 * GATE_CHUNKS)

        def down_done(eng, S, n):
            eng.wait_ge(S.used, n * GCH + S.credit + GCH)

        def passes(eng, layer, group, new_round=None):
            S, M = main[layer], more[layer]
            with eng.Fori(0, NGRP // 2) as i:
                for q in range(2):
                    group(S, i * 2 + q, i * 2 + q, i, q)
            eng.wait_ge(S.added, 1 + 4 * NGRP)
            top = eng.value_load(most[0:1, 0:1], min_val=0, max_val=T)
            with eng.If(top > CAP):
                if new_round:
                    eng.sem_inc(M.added, 1)
                with eng.Fori(0, ROUNDS - 1) as r:
                    if new_round:
                        new_round(shifted[layer])
                    with eng.Fori(0, NGRP // 2) as i:
                        for q in range(2):
                            group(M, r * NGRP + i * 2 + q, i * 2 + q, r * (NGRP // 2) + i, q, (shifted[layer], r))
                eng.wait_ge(M.added, 1 + 4 * NGRP * (ROUNDS - 1))

        block = ctx.enter_context(nc.Block())

        @block.sync
        def _(sp):
            def load_dense(j):
                sp.dma_start(dense_slot(j), dense[j][0]).then_inc(dense_landed[j % SLOTS], 16)

            def load_expert(S, layer, first_group, c):
                j = c % GCH
                e0 = (first_group + c // GCH) * LANES
                if j < 2 * GATE_CHUNKS:
                    w = w_gate if j < GATE_CHUNKS else w_up
                    r0 = (j % GATE_CHUNKS) * 2 * P
                    src = w[layer, bass.ds(e0, LANES), r0:r0 + 2 * P, :].rearrange("e (p r) f -> p e (r f)", r=2)
                else:
                    r0 = (j - 2 * GATE_CHUNKS) * P
                    src = w_down[layer, bass.ds(e0, LANES), r0:r0 + P, :].rearrange("e p n -> p e n")
                dst = ring[:, (TURN + c) % SLOTS, :].rearrange("p (e n) -> p e n", e=LANES)
                sp.dma_start(dst, src).then_inc(S.landed[(TURN + c) % SLOTS], 16)

            for b in range(TB):
                sp.dma_start(h[:, b, :], x[0, b * P:(b + 1) * P, :]).then_inc(x_in, 16)
            load_dense(A_IDX)
            load_dense(W_KV[0])
            sp.dma_start(wr[:, :, :, :], w_router).then_inc(small_in, 16)
            sp.dma_start(brow[0:1, :, :], b_router).then_inc(small_in, 16)
            for layer in range(DEPTH):
                sp.dma_start(psb[:, layer, :, :], p[layer, 0, :, :].rearrange("(b p) c -> p b c", p=P)).then_inc(p_in, 16)
            for j in range(W_Q[0], BEFORE[0]):
                load_dense(j)
            for layer in range(DEPTH):
                S, M = main[layer], more[layer]
                for c in range(SLOTS):
                    j = BEFORE[layer] + c - SLOTS
                    if j >= 0:
                        sp.wait_ge(dense_used, j + 1)
                    load_expert(S, layer, 0, c)
                with sp.Fori(0, NGRP // 2 - 1) as i:
                    for c in range(SLOTS, SLOTS + PAIR):
                        sp.wait_ge(S.used, i * PAIR + (c - SLOTS + 1))
                        load_expert(S, layer, i * 2, c)
                for c in range(SLOTS, PAIR):
                    sp.wait_ge(S.used, (NGRP // 2 - 1) * PAIR + c - SLOTS + 1)
                    load_expert(S, layer, NGRP - 2, c)
                sp.wait_ge(max_ready, layer + 1)
                top = sp.value_load(most[0:1, 0:1], min_val=0, max_val=T)
                with sp.If(top > CAP):
                    sp.wait_ge(S.used, NGRP * GCH)
                    sp.sem_inc(M.used, SLOTS)
                    with sp.Fori(0, ROUNDS - 1) as r:
                        with sp.Fori(0, NGRP // 2) as i:
                            for c in range(PAIR):
                                sp.wait_ge(M.used, r * (NGRP * GCH) + i * PAIR + (c + 1))
                                load_expert(M, layer, i * 2, c)
                    sp.wait_ge(M.used, SLOTS + (ROUNDS - 1) * NGRP * GCH)
                for j in range(BEFORE[layer], BEFORE[layer + 1]):
                    sp.wait_ge(S.used, NGRP * GCH - SLOTS + j - BEFORE[layer] + 1)
                    load_dense(j)
            sp.wait_ge(out_sent, 16 * 2 * TB)

        @block.gpsimd
        def _(pool):
            nc.gpsimd.iota(dist[:, BLK[0]], [[1, P]], base=0, channel_multiplier=-1,
                           allow_small_or_imprecise_dtypes=True).then_inc(consts_ready, 1)
            nc.gpsimd.iota(dist[:, BLK[1]], [[1, T]], base=-P, channel_multiplier=-1,
                           allow_small_or_imprecise_dtypes=True).then_inc(consts_ready, 1)
            nc.gpsimd.iota(iota[:, :], [[1, CAP]], base=0, channel_multiplier=0,
                           allow_small_or_imprecise_dtypes=True).then_inc(consts_ready, 1)
            nc.gpsimd.iota(rev[:, :], [[-1, NE]], base=NE, channel_multiplier=0,
                           allow_small_or_imprecise_dtypes=True).then_inc(consts_ready, 1)
            nc.gpsimd.memset(ones[:, :], 1.0).then_inc(consts_ready, 1)
            for n in range(3 * DEPTH):
                for k, par in enumerate((ln_g, ln_b)):
                    rows = 2 * n + k
                    if rows:
                        pool.wait_ge(lnp_ready, rows)
                    pool.dma_start(lnrow[0:1, :], par[n // 3, n % 3:n % 3 + 1, :]).then_inc(row_in, 16)
                    pool.wait_ge(row_in, 16 * (rows + 1))
                    if n and k == 0:
                        pool.wait_ge(h_ready, 4 * n)
                    nc.gpsimd.partition_broadcast(lnp[:, k, :], lnrow[0:1, :]).then_inc(lnp_ready, 1)

        @block.scalar
        def _(act):
            def copy_hT(event, first_bank):
                for m in range(4):
                    b, j = divmod(m, 2)
                    act.wait_ge(turned, 4 * event + m + 1)
                    nc.scalar.copy(hT[:, 4 * j:4 * j + 4, b * P:(b + 1) * P],
                                   bank[first_bank + m][:, :].rearrange("p (k t) -> p k t", k=4)).then_inc(hT_ready, 1)

            def attention(layer, A):
                if layer == 0:
                    act.wait_ge(dense_used, A_IDX + 1)
                    nc.scalar.copy(iqT, bank[4][:, :].rearrange("p (h t) -> p h t", h=2)).then_inc(A.idx_copied, 1)
                    nc.scalar.copy(ikT, bank[5][:, 0:T]).then_inc(A.idx_copied, 1)
                    nc.scalar.mul(iw, bank[5][:, T:T + TB * IDX_HEADS].rearrange("p (b h) -> p b h", b=TB),
                                  IDX_HEADS ** -0.5).then_inc(A.idx_copied, 1)
                    for n in range(IDX_HEADS):
                        act.wait_ge(A.rel_dot, n // 2 + 1)
                        nc.scalar.activation(relu[:, n, :], bank[n][:, 0:AW], ACT.Relu,
                                             scale=IDX_DIM ** -0.5).then_inc(A.relued, 1)
                act.wait_ge(A.k_dot, 1)
                nc.scalar.copy(kT, bank[6][:, :].rearrange("p (h t) -> p h t", h=2)).then_inc(A.kv_copied, 1)
                act.wait_ge(dense_used, W_KV[layer] + 1)
                nc.scalar.copy(v, bank[7][:, :].rearrange("p (b c) -> p b c", b=TB)).then_inc(A.kv_copied, 1)
                if layer == 0:
                    for n in range(DEPTH):
                        act.wait_ge(p_turned, n + 1)
                        nc.scalar.copy(pT[:, n, :, :], bank[4 + n][:, :].rearrange("p (k t) -> p k t", k=PC)).then_inc(pT_ready, 1)

                def copy_q(n):
                    if n % 4 < 3:
                        act.wait_ge(A.q_dot, n // 4 * 3 + n % 4 + 1)
                    else:
                        act.wait_ge(dense_used, W_Q[layer] + n // 4 + 1)
                    nc.scalar.copy(qT[:, n, :], bank[n % 4][:, 0:T]).then_inc(A.q_copied, 1)

                def exps(n):
                    act.wait_ge(A.peak, 2 * n + 2)
                    for b in range(TB):
                        nc.scalar.activation(prob[:, n % 2, BLK[b]], prob[:, n % 2, BLK[b]], ACT.Exp,
                                             bias=small[:, 2 * n + b:2 * n + b + 1],
                                             accum_out=small[:, 16 + 2 * n + b:17 + 2 * n + b]).then_inc(A.exps, 1)

                def copy_out(n):
                    act.wait_ge(A.pv, n + 1)
                    nc.scalar.copy(qT[:, n, :], bank[7][:, 0:T]).then_inc(A.o_copied, 1)

                for n in range(4):
                    copy_q(n)
                exps(0)
                for n in range(HEADS):
                    if n:
                        copy_out(n - 1)
                    if n + 1 < HEADS:
                        exps(n + 1)
                    if n < 4:
                        copy_q(4 + n)
                    act.wait_ge(A.p_turn, n + 1)
                    nc.scalar.copy(probT, bank[6][:, 0:AW]).then_inc(A.probT_ready, 1)
                copy_out(HEADS - 1)

            def router(layer):
                act.wait_ge(r_exp_in, 2 * layer + 1)
                nc.scalar.activation(gtmp[:, :, :], gtmp[:, :, :], ACT.Exp).then_inc(r_exp, 1)
                act.wait_ge(r_exp_in, 2 * layer + 2)
                nc.scalar.activation(small[:, 40:42], small[:, 40:42], ACT.Exp).then_inc(r_exp, 1)

            def expert_group(S, n, g, turn, q, round_=None):
                for k in range(2):
                    act.wait_ge(S.gathered, n * 2 + (k + 1))
                    nc.scalar.copy(xgT[:, 4 * k:4 * k + 4, :],
                                   bank[k][:, :].rearrange("p (k s) -> p k s", k=4)).then_inc(S.xg, 1)
                gate_done(act, S, n)
                nc.scalar.activation(sig, bank[2][:, :], ACT.Sigmoid).then_inc(S.sigmoid, 1)
                act.wait_ge(S.mturn, n + 1)
                nc.scalar.copy(midT, bank[6][:, :].rearrange("p (c s) -> p c s", c=DOWN_CHUNKS)).then_inc(S.midT, 1)
                down_done(act, S, n)
                for k in range(2):
                    nc.scalar.copy(y[:, k * 512:(k + 1) * 512], bank[4 + k][:, :]).then_inc(S.y, 1)

            copy_hT(0, 0)
            for layer in range(DEPTH):
                attention(layer, attn[layer])
                copy_hT(1 + 3 * layer, 0)
                router(layer)
                passes(act, layer, expert_group)
                copy_hT(2 + 3 * layer, 4)
                for m in range(4):
                    if m < 2:
                        act.wait_ge(gate_dot, 2 * layer + m + 1)
                    else:
                        act.wait_ge(dense_used, W_PLE[layer] + m)
                    nc.scalar.activation(gate[:, m, :], bank[4 + m][:, :], ACT.Sigmoid).then_inc(gate_sig, 1)
                if layer + 1 < DEPTH:
                    copy_hT(3 + 3 * layer, 0)
            for m in range(4):
                b, j = divmod(m, 2)
                act.wait_ge(h_ready, 4 * (3 * DEPTH - 1) + m + 1)
                act.dma_start(out[0, b * P:(b + 1) * P, j * 512:(j + 1) * 512],
                              h[:, b, j * 512:(j + 1) * 512]).then_inc(out_sent, 16)

        @block.vector
        def _(dve):
            steps = [0]
            V = nc.vector

            def link(ins):
                steps[0] += 1
                ins.then_inc(vs, 1)
                dve.wait_ge(vs, steps[0])

            def stats_of(b, j):
                link(V.bn_stats(stats[:, b, j, :], acc[:, b, j * 512:(j + 1) * 512]))

            def layer_norm(n, b):
                mean, var, dev, step = (mv[:, b, i:i + 1] for i in range(4))
                link(V.bn_aggr(mv[:, b, 0:2], stats[:, b, :, :]))
                link(V.tensor_scalar(var, var, EPS, None, ALU.add))
                link(V.tensor_scalar(step.bitcast(I32), var.bitcast(I32), 1, None, ALU.logical_shift_right))
                link(V.tensor_scalar(dev.bitcast(I32), step.bitcast(I32), -1.0, float(0x5F3759DF), ALU.mult, ALU.add))
                for _ in range(3):
                    link(V.scalar_tensor_tensor(step, dev, var, dev, ALU.mult, ALU.mult))
                    link(V.tensor_scalar(step, step, -0.5, 1.5, ALU.mult, ALU.add))
                    link(V.tensor_tensor(dev, dev, step, ALU.mult))
                dve.wait_ge(lnp_ready, 2 * n + 2)
                for j in range(2):
                    c = slice(j * 512, (j + 1) * 512)
                    link(V.scalar_tensor_tensor(h[:, b, c], acc[:, b, c], mean, lnp[:, 0, c], ALU.subtract, ALU.mult))
                    V.scalar_tensor_tensor(h[:, b, c], h[:, b, c], dev, lnp[:, 1, c], ALU.mult, ALU.add).then_inc(h_ready, 1)

            def pick_keys(A):
                dve.wait_ge(A.idx_copied, 3)
                for b in range(TB):
                    for n in range(IDX_HEADS):
                        if b == 0:
                            dve.wait_ge(A.relued, n + 1)
                        before = causal[:, BLK[b]] if n == 0 else score[:, BLK[b]]
                        link(V.scalar_tensor_tensor(score[:, BLK[b]], relu[:, n, BLK[b]], iw[:, b, n:n + 1],
                                                    before, ALU.mult, ALU.add))
                for b in range(TB):
                    for _ in range(TOPK // 8):
                        link(V.max(top8, score[:, BLK[b]]))
                        link(V.match_replace(score[:, BLK[b]], top8, score[:, BLK[b]], TAKEN))
                link(V.tensor_scalar(pen, score, TAKEN, NEG, ALU.is_gt, ALU.mult))
                link(V.tensor_tensor(pen, pen, causal[:, :], ALU.add))

            def attention(layer, A):
                if layer == 0:
                    pick_keys(A)
                mask = pen if layer == 0 else causal[:, :]

                def softmax(n):
                    link(V.scalar_tensor_tensor(bias[:, n % 2, :], dist[:, :], 2.0 ** -(8 * (n + 1) / HEADS), mask,
                                                ALU.mult, ALU.add))
                    dve.wait_ge(A.qk, n + 1)
                    if n >= 2:
                        dve.wait_ge(A.p_turn, n - 1)
                    V.scalar_tensor_tensor(prob[:, n % 2, :], bank[4 + n % 2][:, 0:AW], SCALE, bias[:, n % 2, :],
                                           ALU.mult, ALU.add).then_inc(A.logits, 1)
                    dve.wait_ge(A.logits, n + 1)
                    for b in range(TB):
                        V.tensor_reduce(small[:, 2 * n + b:2 * n + b + 1], prob[:, n % 2, BLK[b]], AX_X, ALU.max,
                                        negate=True).then_inc(A.peak, 1)
                    dve.wait_ge(A.exps, 2 * n + 2)
                    link(V.reciprocal(small[:, 32:34], small[:, 16 + 2 * n:18 + 2 * n]))
                    for b in range(TB):
                        V.tensor_scalar(prob[:, n % 2, BLK[b]], prob[:, n % 2, BLK[b]], small[:, 32 + b:33 + b], None,
                                        ALU.mult).then_inc(A.normed, 1)
                    dve.wait_ge(A.normed, 2 * n + 2)

                for n in range(HEADS):
                    softmax(n)
                for b in range(TB):
                    for j in range(2):
                        if b == 0:
                            dve.wait_ge(mix_dot, 2 * layer + j + 1)
                        else:
                            dve.wait_ge(dense_used, W_O[layer] + j + 1)
                        link(V.scalar_tensor_tensor(acc[:, b, j * 512:(j + 1) * 512], h[:, b, j * 512:(j + 1) * 512],
                                                    ALPHA, bank[2 * b + j][:, :], ALU.mult, ALU.add))
                        stats_of(b, j)
                    layer_norm(3 * layer, b)

            def wide(a, shape):
                return a.broadcast_to(shape)

            def router(layer):
                full = [P, TB, NE]
                dve.wait_ge(router_dot, layer + 1)
                dve.wait_ge(h_ready, 4 * (3 * layer + 1))
                link(V.tensor_copy(lg[:, :, :], bank[4][:, 0:TB * (NG + NE)].rearrange("p (b n) -> p b n", b=TB)))
                g, e = lg[:, :, 0:NG], lg[:, :, NG:]

                def argmax(values, onehot, tmp, width, peak):
                    link(V.tensor_reduce(peak, values, AX_X, ALU.max))
                    each = [P, TB, width]
                    link(V.tensor_tensor(tmp, values, wide(peak.unsqueeze(2), each), ALU.is_equal))
                    link(V.tensor_tensor(tmp, tmp, wide(rev[:, 0:width].unsqueeze(1), each), ALU.mult))
                    link(V.tensor_reduce(small[:, 36:38], tmp, AX_X, ALU.max))
                    link(V.tensor_tensor(onehot, tmp, wide(small[:, 36:38].unsqueeze(2), each), ALU.is_equal))

                argmax(g, gsel[:, :, :], gtmp[:, :, :], NG, small[:, 34:36])
                V.tensor_tensor(gtmp[:, :, :], g, wide(small[:, 34:36].unsqueeze(2), [P, TB, NG]),
                                ALU.subtract).then_inc(r_exp_in, 1)
                four = [P, TB, NG, EPG]
                sel4 = wide(gsel[:, :, :].unsqueeze(3), four)
                em4 = em[:, :, :].rearrange("p b (g e) -> p b g e", g=NG)
                tmp4 = etmp[:, :, :].rearrange("p b (g e) -> p b g e", g=NG)
                link(V.tensor_tensor(em4, e.rearrange("p b (g e) -> p b g e", g=NG), sel4, ALU.mult))
                link(V.tensor_scalar(tmp4, sel4, -NEG, NEG, ALU.mult, ALU.add))
                link(V.tensor_tensor(em[:, :, :], em[:, :, :], etmp[:, :, :], ALU.add))
                argmax(em[:, :, :], first[:, :, :], etmp[:, :, :], NE, small[:, 38:40])
                link(V.scalar_tensor_tensor(em[:, :, :], first[:, :, :], TAKEN, em[:, :, :], ALU.mult, ALU.add))
                argmax(em[:, :, :], second[:, :, :], etmp[:, :, :], NE, small[:, 40:42])
                V.tensor_tensor(assign[:, :, :], first[:, :, :], second[:, :, :], ALU.add).then_inc(routed, 1)
                V.tensor_tensor(small[:, 40:42], small[:, 40:42], small[:, 38:40], ALU.subtract).then_inc(r_exp_in, 1)
                dve.wait_ge(r_exp, 2 * layer + 1)
                link(V.tensor_reduce(small[:, 42:44], gtmp[:, :, :], AX_X, ALU.add))
                dve.wait_ge(r_exp, 2 * layer + 2)
                link(V.tensor_scalar(small[:, 44:46], small[:, 40:42], 1.0, None, ALU.add))
                link(V.tensor_tensor(small[:, 42:44], small[:, 42:44], small[:, 44:46], ALU.mult))
                link(V.reciprocal(small[:, 46:48], small[:, 42:44]))
                link(V.tensor_tensor(small[:, 44:46], small[:, 46:48], small[:, 40:42], ALU.mult))
                link(V.tensor_tensor(weight[:, :, :], first[:, :, :], wide(small[:, 46:48].unsqueeze(2), full), ALU.mult))
                link(V.tensor_tensor(etmp[:, :, :], second[:, :, :], wide(small[:, 44:46].unsqueeze(2), full), ALU.mult))
                link(V.tensor_tensor(weight[:, :, :], weight[:, :, :], etmp[:, :, :], ALU.add))
                dve.wait_ge(ranked, layer + 1)
                dve.wait_ge(routed, layer + 1)
                link(V.scalar_tensor_tensor(rank[:, :, :], bank[5][:, 0:TB * NE].rearrange("p (b e) -> p b e", b=TB), 1.0,
                                            assign[:, :, :], ALU.add, ALU.mult))
                link(V.tensor_scalar(rank[:, :, :], rank[:, :, :], -1.0, None, ALU.add))
                V.tensor_reduce(most[:, :], bank[5][:, TB * NE:(TB + 1) * NE], AX_X, ALU.max).then_inc(max_ready, 1)
                V.tensor_scalar(acc[:, :, :], h[:, :, :], ALPHA, None, ALU.mult).then_inc(main[layer].added, 1)

            def expert_group(S, n, g, turn, q, round_=None):
                four = [P, TB, LANES, CAP]

                def mine(a):
                    return wide(a[:, :, bass.ds(g * LANES, LANES)].unsqueeze(3), four)

                if round_:
                    dve.wait_ge(round_[0], round_[1] + 1)
                V.tensor_tensor(pick, wide(iota[:, :].unsqueeze(1).unsqueeze(1), four), mine(rank), ALU.is_equal).then_inc(S.picked, 1)
                dve.wait_ge(S.picked, n * 2 + 1)
                V.tensor_tensor(wpick, pick, mine(weight), ALU.mult).then_inc(S.picked, 1)
                dve.wait_ge(S.sigmoid, n + 1)
                V.tensor_tensor(half, bank[2][:, :], sig, ALU.mult).then_inc(S.mid, 1)
                dve.wait_ge(S.mid, n * 2 + 1)
                up_done(dve, S, n)
                V.tensor_tensor(mid, half, bank[3][:, :], ALU.mult).then_inc(S.mid, 1)
                dve.wait_ge(S.wturn, n + 1)
                V.tensor_copy(pickT, bank[7][:, 0:T]).then_inc(S.pickT, 1)
                dve.wait_ge(S.added, n * 4 + 1)
                for k in range(4):
                    dve.wait_ge(S.comb, n * 4 + (k + 1))
                    a = acc[:, k // 2, (k % 2) * 512:(k % 2 + 1) * 512]
                    V.tensor_tensor(a, a, bank[k][:, :], ALU.add).then_inc(S.added, 1)

            def next_round(done):
                V.tensor_scalar(rank[:, :, :], rank[:, :, :], -float(CAP), None, ALU.add).then_inc(done, 1)

            dve.wait_ge(consts_ready, 5)
            link(V.tensor_scalar(ident[:, :], dist[:, BLK[0]], 0.0, None, ALU.is_equal))
            link(V.tensor_scalar(tri[:, :], dist[:, BLK[0]], 0.0, None, ALU.is_gt))
            V.tensor_scalar(causal[:, :], dist[:, :], 0.0, NEG, ALU.is_gt, ALU.mult).then_inc(consts_ready, 1)
            dve.wait_ge(consts_ready, 6)
            for layer in range(DEPTH):
                attention(layer, attn[layer])
                router(layer)
                passes(dve, layer, expert_group, next_round)
                for b in range(TB):
                    for j in range(2):
                        stats_of(b, j)
                    layer_norm(3 * layer + 1, b)
                for b in range(TB):
                    for j in range(2):
                        m = 2 * b + j
                        dve.wait_ge(gate_sig, 4 * layer + m + 1)
                        if m < 3:
                            dve.wait_ge(ple_dot, 3 * layer + m + 1)
                        else:
                            dve.wait_ge(dense_used, W_PLE[layer] + 1)
                        link(V.tensor_tensor(gated[:, m, :], bank[m][:, :], gate[:, m, :], ALU.mult))
                        dve.wait_ge(h_ready, 4 * (3 * layer + 1) + m + 1)
                        link(V.scalar_tensor_tensor(acc[:, b, j * 512:(j + 1) * 512], h[:, b, j * 512:(j + 1) * 512],
                                                    ALPHA, gated[:, m, :], ALU.mult, ALU.add))
                        stats_of(b, j)
                    layer_norm(3 * layer + 2, b)

        @block.tensor
        def _(pe):
            mm, transpose = nc.tensor.matmul, nc.tensor.transpose

            def turn(event, first_bank, b):
                for j in range(2):
                    if event == 0:
                        pe.wait_ge(x_in, 16 * TB)
                    else:
                        pe.wait_ge(h_ready, 4 * (event - 1) + 2 * b + j + 1)
                    for k in range(4):
                        ins = transpose(bank[first_bank + 2 * b + j][:, k * P:(k + 1) * P],
                                        h[:, b, (4 * j + k) * P:(4 * j + k + 1) * P], ident[:, :])
                    ins.then_inc(turned, 1)

            def turned_here(event, b):
                pe.wait_ge(hT_ready, 4 * event + 2 * b + 2)

            def columns(o, w, c0, n, tokens=slice(0, T)):
                for k in range(KC):
                    ins = mm(o, w[:, k, c0:c0 + n], hT[:, k, tokens], start=(k == 0), stop=(k == KC - 1))
                return ins

            def rows(o, w, b, c0, n):
                for k in range(KC):
                    ins = mm(o, hT[:, k, b * P:(b + 1) * P], w[:, k, c0:c0 + n], start=(k == 0), stop=(k == KC - 1))
                return ins

            def index_scores(A):
                dense_here(pe, A_IDX)
                w = dense_slot(A_IDX)
                for n in range(2):
                    columns(bank[4][:, n * T:(n + 1) * T], w, n * P, P)
                for k in range(KC):
                    for n in range(2):
                        mm(bank[5][n * IDX_DIM:(n + 1) * IDX_DIM, 0:T], w[:, k, IK0 - IQ0:IW0 - IQ0], hT[:, k, :],
                           start=(k == 0), stop=(k == KC - 1))
                for b in range(TB):
                    ins = rows(bank[5][:, T + b * IDX_HEADS:T + (b + 1) * IDX_HEADS], w, b, IW0 - IQ0, IDX_HEADS)
                ins.then_inc(dense_used, 1)
                pe.wait_ge(A.idx_copied, 3)
                for n in range(0, IDX_HEADS, 2):
                    for b in range(TB):
                        for i in range(2):
                            part = slice(IDX_DIM * i, IDX_DIM * (i + 1))
                            ins = mm(bank[n + i][:, BLK[b]], iqT[part, n // 2, b * P:(b + 1) * P],
                                     ikT[part, 0:P * (b + 1)], start=True, stop=True)
                    ins.then_inc(A.rel_dot, 1)

            def turn_p():
                pe.wait_ge(p_in, 16 * DEPTH)
                for layer in range(DEPTH):
                    for k in range(PC):
                        for b in range(TB):
                            ins = transpose(bank[4 + layer][:, k * T + b * P:k * T + (b + 1) * P],
                                            psb[:, layer, b, k * P:(k + 1) * P], ident[:, :])
                    ins.then_inc(p_turned, 1)

            def attention(layer, A, event):
                if layer == 0:
                    for b in range(TB):
                        turned_here(event, b)
                    index_scores(A)
                j = W_KV[layer]
                dense_here(pe, j)
                w = dense_slot(j)
                for b in range(TB):
                    tokens = slice(b * P, (b + 1) * P)
                    turned_here(event, b)
                    for n in range(KV_HEADS):
                        ins = columns(bank[6][:, n * T + b * P:n * T + (b + 1) * P], w, n * P, P, tokens)
                    if b == TB - 1:
                        ins.then_inc(A.k_dot, 1)
                    ins = rows(bank[7][:, b * KV:(b + 1) * KV], w, b, KV, KV)
                ins.then_inc(dense_used, 1)
                if layer == 0:
                    turn_p()
                    pe.wait_ge(A.relued, IDX_HEADS)

                def project_q(n):
                    j = W_Q[layer] + n // 4
                    if n % 4 == 0:
                        dense_here(pe, j)
                    if n >= 4:
                        pe.wait_ge(A.q_copied, n - 3)
                    ins = columns(bank[n % 4][:, 0:T], dense_slot(j), (n % 4) * P, P)
                    ins.then_inc(dense_used if n % 4 == 3 else A.q_dot, 1)

                def qk(n):
                    pe.wait_ge(A.q_copied, n + 1)
                    if n >= 2:
                        pe.wait_ge(A.logits, n - 1)
                    for b in range(TB):
                        ins = mm(bank[4 + n % 2][:, BLK[b]], qT[:, n, b * P:(b + 1) * P],
                                 kT[:, n // GROUP, 0:P * (b + 1)], start=True, stop=True)
                    ins.then_inc(A.qk, 1)

                def turn_prob(n):
                    pe.wait_ge(A.normed, 2 * n + 2)
                    if n:
                        pe.wait_ge(A.probT_ready, n)
                    for k in range(3):
                        ins = transpose(bank[6][:, k * P:(k + 1) * P], prob[:, n % 2, k * P:(k + 1) * P], ident[:, :])
                    ins.then_inc(A.p_turn, 1)

                def pv(n):
                    pe.wait_ge(A.probT_ready, n + 1)
                    if n:
                        pe.wait_ge(A.o_copied, n)
                    o, hd = bank[7], slice(n // GROUP * HD, (n // GROUP + 1) * HD)
                    mm(o[:, 0:T], v[:, 0, hd], probT[:, 0:T], start=True, stop=False)
                    mm(o[:, P:T], v[:, 1, hd], probT[:, T:AW], start=False, stop=True).then_inc(A.pv, 1)

                def mix(m, heads):
                    b, half_ = divmod(m, 2)
                    dense_here(pe, W_O[layer] + half_)
                    for n in heads:
                        pe.wait_ge(A.o_copied, n + 1)
                        ins = mm(bank[m][:, :], qT[:, n, b * P:(b + 1) * P], dense_slot(W_O[layer] + half_)[:, n, :],
                                 start=(n == 0), stop=(n == HEADS - 1))
                    return ins

                for n in range(4):
                    project_q(n)
                pe.wait_ge(A.kv_copied, 2)
                if layer == 0:
                    pe.wait_ge(pT_ready, DEPTH)
                qk(0)
                for n in range(HEADS):
                    if n + 1 < HEADS:
                        qk(n + 1)
                    if n:
                        pv(n - 1)
                    if n < 4:
                        project_q(4 + n)
                    else:
                        pe.wait_ge(A.q_copied, n + 1)
                        mix(n - 4, range(4))
                    turn_prob(n)
                pv(HEADS - 1)
                for m in range(4):
                    mix(m, range(4, HEADS)).then_inc((mix_dot, dense_used)[m // 2], 1)

            def router(layer, event):
                for b in range(TB):
                    turned_here(event, b)
                    o = bank[4][:, b * (NG + NE):(b + 1) * (NG + NE)]
                    for k in range(KC):
                        mm(o, hT[:, k, b * P:(b + 1) * P], wr[:, layer, k, :], start=(k == 0), stop=False)
                    ins = mm(o, ones[0:1, :], brow[0:1, layer, :], start=False, stop=True)
                ins.then_inc(router_dot, 1)
                pe.wait_ge(routed, layer + 1)
                mm(bank[5][:, 0:NE], tri[:, :], assign[:, 0, :], start=True, stop=True)
                mm(bank[5][:, NE:2 * NE], ones[:, :], assign[:, 0, :], start=True, stop=False)
                mm(bank[5][:, NE:2 * NE], tri[:, :], assign[:, 1, :], start=False, stop=True)
                for b in range(TB):
                    ins = mm(bank[5][:, 2 * NE:3 * NE], ones[:, :], assign[:, b, :], start=(b == 0), stop=(b == 1))
                ins.then_inc(ranked, 1)

            def expert_group(S, n, g, turn, q, round_=None):
                pe.wait_ge(S.picked, n * 2 + 1)
                pe.wait_ge(S.added, n * 4 + 1)
                for k in range(KC):
                    r0 = k // 2 * 2 * P
                    r = h[:, :, r0:r0 + 2 * P].rearrange("p b (d r) -> p b r d", r=2)
                    for b in range(TB):
                        ins = mm(bank[k // 4][:, (k % 4) * P:(k % 4 + 1) * P], r[:, b, k % 2, :],
                                 pick[:, b].rearrange("p e s -> p (e s)"), start=(b == 0), stop=(b == 1))
                    if k % 4 == 3:
                        ins.then_inc(S.gathered, 1)
                pe.wait_ge(S.picked, n * 2 + 2)
                for b in range(TB):
                    ins = transpose(bank[7][:, b * P:(b + 1) * P], wpick[:, b].rearrange("p e s -> p (e s)"), ident[:, :])
                ins.then_inc(S.wturn, 1)
                pe.wait_ge(S.xg, n * 2 + 2)
                c = q * GCH
                for o in (bank[2], bank[3]):
                    for k in range(KC):
                        if k % 2 == 0:
                            expert_here(pe, S, turn, c)
                        for e in range(LANES):
                            lane = slice(e * CAP, (e + 1) * CAP)
                            ins = mm(o[lane, :], xgT[:, k, lane], expert_slot(c)[:, e, k % 2, :],
                                     start=(k == 0), stop=(k == KC - 1))
                        if k % 2:
                            ins.then_inc(S.used, 1)
                            c += 1
                pe.wait_ge(S.mid, n * 2 + 2)
                for k in range(DOWN_CHUNKS):
                    ins = transpose(bank[6][:, k * P:(k + 1) * P], mid[:, k * P:(k + 1) * P], ident[:, :])
                ins.then_inc(S.mturn, 1)
                pe.wait_ge(S.midT, n + 1)
                for k in range(DOWN_CHUNKS):
                    expert_here(pe, S, turn, c)
                    for half_ in range(2):
                        for e in range(LANES):
                            lane = slice(e * CAP, (e + 1) * CAP)
                            ins = mm(bank[4 + half_][lane, :], midT[:, k, lane],
                                     expert_slot(c)[:, e, half_ * 512:(half_ + 1) * 512],
                                     start=(k == 0), stop=(k == DOWN_CHUNKS - 1))
                    ins.then_inc(S.used, 1)
                    c += 1
                pe.wait_ge(S.pickT, n + 1)
                pe.wait_ge(S.y, n * 2 + 2)
                for k in range(4):
                    b, half_ = k // 2, k % 2
                    mm(bank[k][:, :], pickT[:, b * P:(b + 1) * P], y[:, half_ * 512:(half_ + 1) * 512],
                       start=True, stop=True).then_inc(S.comb, 1)

            pe.wait_ge(consts_ready, 6)
            for b in range(TB):
                turn(0, 0, b)
            for layer in range(DEPTH):
                event = 3 * layer
                attention(layer, attn[layer], event)
                pe.wait_ge(small_in, 32)
                for b in range(TB):
                    turn(event + 1, 0, b)
                router(layer, event + 1)
                passes(pe, layer, expert_group)
                dense_here(pe, W_PLE[layer])
                for m in range(4):
                    b, j = divmod(m, 2)
                    for c in range(PC):
                        ins = mm(bank[m][:, :], pT[:, layer, c, b * P:(b + 1) * P],
                                 dense_slot(W_PLE[layer])[:, c, j * 512:(j + 1) * 512], start=(c == 0), stop=(c == PC - 1))
                    ins.then_inc(ple_dot if m < 3 else dense_used, 1)
                turn(event + 2, 4, 0)
                for b in range(TB):
                    turned_here(event + 2, b)
                    for j in range(2):
                        dense_here(pe, W_PLE[layer] + 1 + j)
                        rows(bank[4 + 2 * b + j][:, :], dense_slot(W_PLE[layer] + 1 + j), b, 0, 512)\
                            .then_inc((gate_dot, dense_used)[b], 1)
                        if b == 0 and j == 0:
                            turn(event + 2, 4, 1)
                    if layer + 1 < DEPTH and b == 1:
                        turn(event + 3, 0, 0)
                if layer + 1 < DEPTH:
                    turn(event + 3, 0, 1)


INPUTS = ["x", "p", "w_in_a", "w_o_a", "w_kv_shared", "w_q_b", "w_o_b", "w_router", "b_router", "w_gate", "w_up", "w_down", "w_ple", "w_ple_gate", "ln_g", "ln_b"]


def kernel(**inputs):
    import numpy as np
    import concourse.bacc as bacc
    from concourse.bass_utils import run_bass_kernel_spmd

    nc = bacc.Bacc("TRN2", target_bir_lowering=False, num_devices=1)
    w = np.concatenate([inputs["w_router_group"], inputs["w_router_expert"]], axis=2)
    inputs["w_router"] = w.reshape(DEPTH, KC, P, NG + NE).transpose(2, 0, 1, 3)
    inputs["b_router"] = np.concatenate([inputs["b_router_group"], inputs["b_router_expert"]], axis=1)[None]
    arrays, args = {}, []
    for name in INPUTS:
        a = np.ascontiguousarray(inputs[name])
        arrays[f"in_{name}"] = a
        args.append(nc.dram_tensor(f"in_{name}", a.shape, mybir.dt.from_np(a.dtype), kind="ExternalInput").ap())
    args.append(nc.dram_tensor("out_h", (1, T, D), F32, kind="ExternalOutput").ap())
    trunk(nc, *args)
    r = run_bass_kernel_spmd(nc, [arrays], core_ids=[0])
    return r.results[0]["out_h"]
```

```python
from contextlib import ExitStack

import concourse.bass as bass
from concourse import mybir

ALU = mybir.AluOpType
ACT = mybir.ActivationFunctionType
F32 = mybir.dt.float32
I32 = mybir.dt.int32
AX_X = mybir.AxisListType.X

P = 128
T = 256
TB = T // P
D = 1024
KC = D // P
DEPTH = 2
HEADS, KV_HEADS, HD = 8, 2, 128
GROUP = HEADS // KV_HEADS
KV = KV_HEADS * HD
IDX_HEADS, IDX_DIM = 4, 64
TOPK = min(256, T // 4)
NG, EPG = 4, 8
NE = NG * EPG
F = 512
PLE = 256
PC = PLE // P
ALPHA = (2.0 * DEPTH) ** 0.25
EPS = 1e-5
SCALE = HD ** -0.5
NEG = -1e30
TAKEN = -3e38

AW = P + T
BLK = (slice(0, P), slice(P, AW))

LANES = 4
CAP = P // LANES
ROUNDS = -(-T // CAP)
NGRP = NE // LANES
GATE_CHUNKS = D // (2 * P)
DOWN_CHUNKS = F // P
ADDS = 6
GCH = 2 * GATE_CHUNKS + DOWN_CHUNKS
SCRATCH = 6544
SLOTS = 8
SLOT = 4096
PAIR = 2 * GCH
assert PAIR % SLOTS == 0 and NGRP % 2 == 0

Q0, K0, V0 = 0, D, D + KV
IQ0 = D + 2 * KV
IK0 = IQ0 + IDX_HEADS * IDX_DIM
IW0 = IK0 + IDX_DIM
A_COLS = IW0 + IDX_HEADS
IDXW = A_COLS - IQ0


def trunk(nc, x, p, w_in_a, w_o_a, w_kv, w_q_b, w_o_b, w_router, b_router,
          w_gate, w_up, w_down, w_ple, w_pg, ln_g, ln_b, out):
    with ExitStack() as ctx:
        def sb(name, shape, dt=F32):
            return ctx.enter_context(nc.sbuf_tensor(name, shape, dt))

        def sem(name):
            return ctx.enter_context(nc.semaphore(name))

        bank = [ctx.enter_context(nc.psum_tensor(f"bank{i}", [P, 512], F32)) for i in range(8)]

        ring = sb("ring", [P, SLOTS, SLOT])
        h = sb("h", [P, TB, D])
        acc = sb("acc", [P, TB, D])
        hT = sb("hT", [P, KC, T])
        lnp = sb("lnp", [P, 2, D])
        lnrow = sb("lnrow", [1, 2, D])
        scratch = sb("scratch", [P, SCRATCH])
        pT = sb("pT", [P, DEPTH, PC, T])
        wr = sb("wr", [P, DEPTH, KC, NG + NE])
        brow = sb("brow", [1, DEPTH, NG + NE])
        ident = sb("ident", [P, P])
        tri = sb("tri", [P, P])
        ones = sb("ones", [P, P])
        dist = sb("dist", [P, AW])
        causal = sb("causal", [P, AW])
        iota = sb("iota", [P, CAP])
        rev = sb("rev", [P, NE])
        small = sb("small", [P, 64])
        stats = sb("stats", [P, TB, 2, 6])
        mv = sb("mv", [P, TB, 7])
        route = sb("route", [P, TB, 20])
        lg = sb("lg", [P, TB, NG + NE])
        gpen = sb("gpen", [P, TB, NG])
        gexp = sb("gexp", [P, TB, NG])
        em = sb("em", [P, TB, NE])
        etmp = sb("etmp", [P, TB, NE])
        etmp2 = sb("etmp2", [P, TB, NE])
        first = sb("first", [P, TB, NE])
        second = sb("second", [P, TB, NE])
        assign = sb("assign", [P, TB, NE])
        weight = sb("weight", [P, TB, NE])
        rank = sb("rank", [P, TB, NE + LANES])
        most = sb("most", [P, 1], I32)

        at = [0]

        def view(n):
            at[0] += n
            assert at[0] <= SCRATCH
            return scratch[:, at[0] - n:at[0]]

        qT = view(HEADS * T).rearrange("p (h t) -> p h t", h=HEADS)
        kT = view(KV_HEADS * T).rearrange("p (h t) -> p h t", h=KV_HEADS)
        v = view(TB * KV).rearrange("p (b c) -> p b c", b=TB)
        iqT = view(2 * T).rearrange("p (h t) -> p h t", h=2)
        ikT = view(T)
        iwT = view(T)[IDX_DIM:IDX_DIM + IDX_HEADS, :]
        at[0] -= T
        iw = view(TB * IDX_HEADS).rearrange("p (b h) -> p b h", b=TB)
        score = view(AW)
        pen = view(AW)
        bias = view(2 * AW).rearrange("p (n c) -> p n c", n=2)
        prob = view(2 * AW).rearrange("p (n c) -> p n c", n=2)
        probT = view(AW)
        top8 = view(8)
        at[0] -= 5 * AW + 8
        relu = view(4 * AW).rearrange("p (n c) -> p n c", n=4)
        at[0] = 0
        xgT = view(KC * P).rearrange("p (k s) -> p k s", k=KC)
        pick = view(TB * P).rearrange("p (b e s) -> p b e s", b=TB, e=LANES)
        wpick = view(TB * P).rearrange("p (b e s) -> p b e s", b=TB, e=LANES)
        pickT = view(T)
        sig = view(F)
        half = view(F)
        mid = view(F)
        midT = view(F).rearrange("p (c s) -> p c s", c=DOWN_CHUNKS)
        y = view(D)
        at[0] = 0
        gate = view(4 * 512).rearrange("p (n c) -> p n c", n=4)
        gated = view(4 * 512).rearrange("p (n c) -> p n c", n=4)
        at[0] = 0
        psb = view(DEPTH * TB * PLE).rearrange("p (l b c) -> p l b c", l=DEPTH, b=TB)

        x_in = [sem(f"x_in{b}") for b in range(TB)]
        small_in, p_in = sem("small_in"), sem("p_in")
        row_in = [sem("gain_row_in"), sem("shift_row_in")]
        lnp_ready = sem("lnp_ready")
        vs = sem("vector_step")
        consts_ready = sem("consts_ready")
        dense_landed = [sem(f"dense_landed{i}") for i in range(SLOTS)]
        dense_used = sem("dense_used")
        mean_ready, centered, gained, h_ready = sem("mean_ready"), sem("centered"), sem("gained"), sem("h_ready")
        turned = sem("turned")
        hT_ready = sem("hT_ready")
        p_turned, pT_ready = sem("p_turned"), sem("pT_ready")
        routed, router_dot = sem("routed"), sem("router_dot")
        ranked = sem("ranked")
        r_exp_in, r_exp = sem("router_exp_in"), sem("router_exp")
        max_ready = sem("max_ready")
        idx_copied, iw_turned, rel_dot, relued = sem("idx_copied"), sem("iw_turned"), sem("rel_dot"), sem("relued")
        ple_dot, gate_dot, gate_sig = sem("ple_dot"), sem("gate_dot"), sem("gate_sig")
        mix_dot, out_sent = sem("mix_dot"), sem("out_sent")

        class Attention:

            def __init__(self, layer):
                self.k_dot = sem(f"k_dot_{layer}")
                self.q_dot = sem(f"q_dot_{layer}")
                self.kv_copied = sem(f"kv_copied_{layer}")
                self.q_copied = sem(f"q_copied_{layer}")
                self.qk = sem(f"qk_{layer}")
                self.logits = sem(f"logits_{layer}")
                self.peak = sem(f"peak_{layer}")
                self.exps = sem(f"exps_{layer}")
                self.normed = sem(f"normed_{layer}")
                self.p_turn = sem(f"p_turn_{layer}")
                self.probT_ready = sem(f"probT_ready_{layer}")
                self.pv = sem(f"pv_{layer}")
                self.o_copied = sem(f"o_copied_{layer}")

        class Pass:

            def __init__(self, name, credit):
                self.credit = credit
                self.landed = [sem(f"landed{i}_{name}") for i in range(SLOTS)]
                self.used = sem(f"used_{name}")
                self.picked = sem(f"picked_{name}")
                self.gathered = sem(f"gathered_{name}")
                self.xg = sem(f"xg_{name}")
                self.sigmoid = sem(f"sigmoid_{name}")
                self.mid = sem(f"mid_{name}")
                self.wturn = sem(f"wturn_{name}")
                self.pickT = sem(f"pickT_{name}")
                self.mturn = sem(f"mturn_{name}")
                self.midT = sem(f"midT_{name}")
                self.y = sem(f"y_{name}")
                self.down_half = sem(f"down_half_{name}")
                self.comb = sem(f"comb_{name}")
                self.added = sem(f"added_{name}")

        attn = [Attention(layer) for layer in range(DEPTH)]
        main = [Pass(f"main{layer}", 0) for layer in range(DEPTH)]
        more = [Pass(f"more{layer}", SLOTS) for layer in range(DEPTH)]
        shifted = [sem(f"shifted{layer}") for layer in range(DEPTH)]

        def cols(w, c0, n):
            return w[:, c0:c0 + n].rearrange("(k p) n -> p k n", p=P), KC, n

        dense = [cols(w_in_a[0], IQ0, IDXW), cols(w_in_a[0], K0, 2 * KV), cols(w_in_a[0], Q0, 512),
                 cols(w_in_a[0], Q0 + 512, 512), cols(w_o_a[0], 0, 512), cols(w_o_a[0], 512, 512),
                 (w_ple[0].rearrange("(k p) n -> p k n", p=P), PC, D), cols(w_pg[0], 0, 512),
                 cols(w_pg[0], 512, 512), cols(w_kv, 0, 2 * KV), cols(w_q_b[0], 0, 512),
                 cols(w_q_b[0], 512, 512), cols(w_o_b[0], 0, 512), cols(w_o_b[0], 512, 512),
                 (w_ple[1].rearrange("(k p) n -> p k n", p=P), PC, D), cols(w_pg[1], 0, 512),
                 cols(w_pg[1], 512, 512)]
        A_IDX = 0
        W_KV, W_Q, W_O, W_PLE = (1, 9), (2, 10), (4, 12), (6, 14)
        K_BANK = (6, 4)
        BEFORE = (6, 14, len(dense))
        TURN = BEFORE[0] % SLOTS
        assert all(n % SLOTS == TURN for n in BEFORE[:DEPTH]) and len(dense) - BEFORE[1] <= SLOTS

        def dense_slot(j):
            return ring[:, j % SLOTS, 0:dense[j][1] * dense[j][2]].rearrange("p (k n) -> p k n", n=dense[j][2])

        def dense_here(eng, j):
            eng.wait_ge(dense_landed[j % SLOTS], 16 * (j // SLOTS + 1))

        def expert_slot(c):
            s = ring[:, (TURN + c) % SLOTS, :]
            if c % GCH < 2 * GATE_CHUNKS:
                return s.rearrange("p (e r f) -> p e r f", e=LANES, r=2)
            return s.rearrange("p (e n) -> p e n", e=LANES)

        def expert_here(eng, S, turn, c):
            eng.wait_ge(S.landed[(TURN + c) % SLOTS], turn * (16 * (PAIR // SLOTS)) + 16 * (c // SLOTS + 1))

        def gather_bank(c):
            return bank[c % 2][:, c // 2 * 2 * P:(c // 2 + 1) * 2 * P]

        def gate_done(eng, S, n):
            eng.wait_ge(S.used, n * GCH + S.credit + GATE_CHUNKS)

        def up_done(eng, S, n):
            eng.wait_ge(S.used, n * GCH + S.credit + 2 * GATE_CHUNKS)

        def down_done(eng, S, n):
            eng.wait_ge(S.used, n * GCH + S.credit + GCH)

        def passes(eng, layer, group, new_round=None):
            S, M = main[layer], more[layer]
            with eng.Fori(0, NGRP // 2) as i:
                group(S, i * 2, i * 2, i, 0, 0)
                eng.wait_ge(max_ready, layer + 1)
                top = eng.value_load(most[0:1, 0:1], min_val=0, max_val=T)
                group(S, i * 2 + 1, i * 2 + 1, i, 1, 0)
            if new_round:
                eng.wait_ge(S.added, TB + ADDS * NGRP)
            with eng.If(top > CAP):
                if new_round:
                    eng.sem_inc(M.added, TB)
                with eng.Fori(0, ROUNDS - 1) as r:
                    if new_round:
                        new_round(M, shifted[layer], r)
                    with eng.Fori(0, NGRP // 2) as i:
                        for q in range(2):
                            group(M, r * NGRP + i * 2 + q, i * 2 + q, r * (NGRP // 2) + i, q, r)
                eng.wait_ge(M.added, TB + ADDS * NGRP * (ROUNDS - 1))

        block = ctx.enter_context(nc.Block())

        @block.sync
        def _(sp):
            def load_dense(j):
                sp.dma_start(dense_slot(j), dense[j][0]).then_inc(dense_landed[j % SLOTS], 16)

            def load_expert(S, layer, first_group, c):
                j = c % GCH
                e0 = (first_group + c // GCH) * LANES
                if j < 2 * GATE_CHUNKS:
                    w = w_gate if j < GATE_CHUNKS else w_up
                    r0 = (j % GATE_CHUNKS) * 2 * P
                    src = w[layer, bass.ds(e0, LANES), r0:r0 + 2 * P, :].rearrange("e (p r) f -> p e (r f)", r=2)
                else:
                    r0 = (j - 2 * GATE_CHUNKS) * P
                    src = w_down[layer, bass.ds(e0, LANES), r0:r0 + P, :].rearrange("e p n -> p e n")
                dst = ring[:, (TURN + c) % SLOTS, :].rearrange("p (e n) -> p e n", e=LANES)
                sp.dma_start(dst, src).then_inc(S.landed[(TURN + c) % SLOTS], 16)

            for b in range(TB):
                sp.dma_start(h[:, b, :], x[0, b * P:(b + 1) * P, :]).then_inc(x_in[b], 16)
            load_dense(A_IDX)
            load_dense(W_KV[0])
            sp.dma_start(wr[:, :, :, :], w_router).then_inc(small_in, 16)
            sp.dma_start(brow[0:1, :, :], b_router).then_inc(small_in, 16)
            for layer in range(DEPTH):
                sp.dma_start(psb[:, layer, :, :], p[layer, 0, :, :].rearrange("(b p) c -> p b c", p=P)).then_inc(p_in, 16)
            for j in range(W_Q[0], BEFORE[0]):
                load_dense(j)
            for layer in range(DEPTH):
                S, M = main[layer], more[layer]
                for c in range(SLOTS):
                    j = BEFORE[layer] + c - SLOTS
                    if j >= 0:
                        sp.wait_ge(dense_used, j + 1)
                    load_expert(S, layer, 0, c)
                with sp.Fori(0, NGRP // 2 - 1) as i:
                    for c in range(SLOTS, SLOTS + PAIR):
                        sp.wait_ge(S.used, i * PAIR + (c - SLOTS + 1))
                        load_expert(S, layer, i * 2, c)
                for c in range(SLOTS, PAIR):
                    sp.wait_ge(S.used, (NGRP // 2 - 1) * PAIR + c - SLOTS + 1)
                    load_expert(S, layer, NGRP - 2, c)
                sp.wait_ge(max_ready, layer + 1)
                top = sp.value_load(most[0:1, 0:1], min_val=0, max_val=T)
                with sp.If(top > CAP):
                    sp.wait_ge(S.used, NGRP * GCH)
                    sp.sem_inc(M.used, SLOTS)
                    with sp.Fori(0, ROUNDS - 1) as r:
                        with sp.Fori(0, NGRP // 2) as i:
                            for c in range(PAIR):
                                sp.wait_ge(M.used, r * (NGRP * GCH) + i * PAIR + (c + 1))
                                load_expert(M, layer, i * 2, c)
                    sp.wait_ge(M.used, SLOTS + (ROUNDS - 1) * NGRP * GCH)
                for j in range(BEFORE[layer], BEFORE[layer + 1]):
                    sp.wait_ge(S.used, NGRP * GCH - SLOTS + j - BEFORE[layer] + 1)
                    load_dense(j)
            sp.wait_ge(out_sent, 16 * 2 * TB)

        @block.gpsimd
        def _(pool):
            nc.gpsimd.iota(dist[:, BLK[0]], [[1, P]], base=0, channel_multiplier=-1,
                           allow_small_or_imprecise_dtypes=True).then_inc(consts_ready, 1)
            nc.gpsimd.iota(dist[:, BLK[1]], [[1, T]], base=-P, channel_multiplier=-1,
                           allow_small_or_imprecise_dtypes=True).then_inc(consts_ready, 1)
            nc.gpsimd.iota(iota[:, :], [[1, CAP]], base=1, channel_multiplier=0,
                           allow_small_or_imprecise_dtypes=True).then_inc(consts_ready, 1)
            nc.gpsimd.iota(rev[:, :], [[-1, NE]], base=NE, channel_multiplier=0,
                           allow_small_or_imprecise_dtypes=True).then_inc(consts_ready, 1)
            nc.gpsimd.memset(ones[:, :], 1.0).then_inc(consts_ready, 1)
            def load_rows(n):
                for k, par in enumerate((ln_g, ln_b)):
                    if n:
                        pool.wait_ge(lnp_ready, 2 * n - 1 + k)
                    pool.dma_start(lnrow[0:1, k, :], par[n // 3, n % 3:n % 3 + 1, :]).then_inc(row_in[k], 16)

            load_rows(0)
            for n in range(3 * DEPTH):
                if n:
                    pool.wait_ge(h_ready, 4 * n)
                for k in range(2):
                    pool.wait_ge(row_in[k], 16 * (n + 1))
                    nc.gpsimd.partition_broadcast(lnp[:, k, :], lnrow[0:1, k, :]).then_inc(lnp_ready, 1)
                if n + 1 < 3 * DEPTH:
                    load_rows(n + 1)
                pool.wait_ge(lnp_ready, 2 * n + 1)
                for m in range(4):
                    b, j = divmod(m, 2)
                    c = slice(j * 512, (j + 1) * 512)
                    pool.wait_ge(centered, 4 * n + m + 1)
                    nc.gpsimd.tensor_tensor(h[:, b, c], h[:, b, c], lnp[:, 0, c], ALU.mult).then_inc(gained, 1)

        @block.scalar
        def _(act):
            def center(n, b):
                act.wait_ge(mean_ready, TB * n + b + 1)
                for j in range(2):
                    c = slice(j * 512, (j + 1) * 512)
                    nc.scalar.activation(h[:, b, c], acc[:, b, c], ACT.Identity, bias=mv[:, b, 6:7]).then_inc(centered, 1)

            def copy_hT(event, first_bank, b):
                for j in range(2):
                    m = 2 * b + j
                    act.wait_ge(turned, 4 * event + m + 1)
                    nc.scalar.copy(hT[:, 4 * j:4 * j + 4, b * P:(b + 1) * P],
                                   bank[first_bank + m][:, :].rearrange("p (k t) -> p k t", k=4)).then_inc(hT_ready, 1)

            def attention(layer, A):
                if layer == 0:
                    act.wait_ge(dense_used, A_IDX + 1)
                    nc.scalar.copy(iqT, bank[4][:, :].rearrange("p (h t) -> p h t", h=2)).then_inc(idx_copied, 1)
                    for i in range(2):
                        nc.scalar.copy(ikT[i * IDX_DIM:(i + 1) * IDX_DIM, :], bank[5][0:IDX_DIM, 0:T]).then_inc(idx_copied, 1)
                    nc.scalar.mul(iwT, bank[5][IDX_DIM:IDX_DIM + IDX_HEADS, 0:T], IDX_HEADS ** -0.5).then_inc(idx_copied, 1)
                    act.wait_ge(iw_turned, 1)
                    nc.scalar.copy(iw, bank[5][:, 0:TB * IDX_HEADS].rearrange("p (b h) -> p b h", b=TB)).then_inc(idx_copied, 1)
                    for n in range(IDX_HEADS):
                        act.wait_ge(rel_dot, n // 2 + 1)
                        nc.scalar.activation(relu[:, n, :], bank[n][:, 0:AW], ACT.Relu,
                                             scale=IDX_DIM ** -0.5).then_inc(relued, 1)
                act.wait_ge(A.k_dot, 1)
                nc.scalar.copy(kT, bank[K_BANK[layer]][:, :].rearrange("p (h t) -> p h t", h=2)).then_inc(A.kv_copied, 1)
                act.wait_ge(dense_used, W_KV[layer] + 1)
                nc.scalar.copy(v, bank[K_BANK[layer] + 1][:, :].rearrange("p (b c) -> p b c", b=TB)).then_inc(A.kv_copied, 1)
                if layer == 0:
                    for n in range(DEPTH):
                        act.wait_ge(p_turned, n + 1)
                        nc.scalar.copy(pT[:, n, :, :], bank[4 + n][:, :].rearrange("p (k t) -> p k t", k=PC)).then_inc(pT_ready, 1)

                def copy_q(n):
                    if n % 4 < 3:
                        act.wait_ge(A.q_dot, n // 4 * 3 + n % 4 + 1)
                    else:
                        act.wait_ge(dense_used, W_Q[layer] + n // 4 + 1)
                    nc.scalar.copy(qT[:, n, :], bank[n % 4][:, 0:T]).then_inc(A.q_copied, 1)

                def exps(n):
                    act.wait_ge(A.peak, 2 * n + 2)
                    for b in range(TB):
                        nc.scalar.activation(prob[:, n % 2, BLK[b]], prob[:, n % 2, BLK[b]], ACT.Exp,
                                             bias=small[:, 2 * n + b:2 * n + b + 1],
                                             accum_out=small[:, 16 + 2 * n + b:17 + 2 * n + b]).then_inc(A.exps, 1)

                def copy_out(n):
                    act.wait_ge(A.pv, n + 1)
                    nc.scalar.copy(qT[:, n, :], bank[7][:, 0:T]).then_inc(A.o_copied, 1)

                for n in range(4):
                    copy_q(n)
                    if n == 2:
                        exps(0)
                for n in range(HEADS):
                    if n:
                        copy_out(n - 1)
                    if n + 1 < HEADS:
                        exps(n + 1)
                    if n < 4:
                        copy_q(4 + n)
                    act.wait_ge(A.p_turn, n + 1)
                    nc.scalar.copy(probT, bank[6][:, 0:AW]).then_inc(A.probT_ready, 1)
                copy_out(HEADS - 1)

            def before_experts(layer):
                event = 3 * layer + 1
                for b in range(TB):
                    center(event - 1, b)
                    copy_hT(event, 0, b)
                    act.wait_ge(h_ready, 4 * (event - 1) + 2 * b + 2)
                    nc.scalar.mul(acc[:, b, :], h[:, b, :], ALPHA).then_inc(main[layer].added, 1)
                for b in range(TB):
                    R = route[:, b, :]
                    act.wait_ge(r_exp_in, 4 * layer + 2 * b + 1)
                    nc.scalar.activation(gexp[:, b, :], lg[:, b, 0:NG], ACT.Exp,
                                         bias=R[:, 9:10], accum_out=R[:, 12:13]).then_inc(r_exp, 1)
                    act.wait_ge(r_exp_in, 4 * layer + 2 * b + 2)
                    nc.scalar.activation(R[:, 13:14], R[:, 0:1], ACT.Exp, bias=R[:, 1:2], scale=-1.0).then_inc(r_exp, 1)

            def expert_group(S, n, g, turn, q, r):
                for c in range(GATE_CHUNKS):
                    act.wait_ge(S.gathered, n * GATE_CHUNKS + (c + 1))
                    nc.scalar.copy(xgT[:, 2 * c:2 * c + 2, :], gather_bank(c).rearrange("p (k s) -> p k s", k=2)).then_inc(S.xg, 1)
                gate_done(act, S, n)
                nc.scalar.activation(sig, bank[2][:, :], ACT.Sigmoid).then_inc(S.sigmoid, 1)
                act.wait_ge(S.mturn, n + 1)
                nc.scalar.copy(midT, bank[6][:, :].rearrange("p (c s) -> p c s", c=DOWN_CHUNKS)).then_inc(S.midT, 1)
                for k in range(2):
                    if k == 0:
                        act.wait_ge(S.down_half, n + 1)
                    else:
                        down_done(act, S, n)
                    nc.scalar.copy(y[:, k * 512:(k + 1) * 512], bank[4 + k][:, :]).then_inc(S.y, 1)

            def embedding(layer):
                for b in range(TB):
                    center(1 + 3 * layer, b)
                    copy_hT(2 + 3 * layer, 4, b)
                for m in range(4):
                    if m < 2:
                        act.wait_ge(gate_dot, 2 * layer + m + 1)
                    else:
                        act.wait_ge(dense_used, W_PLE[layer] + m)
                    nc.scalar.activation(gate[:, m, :], bank[4 + m][:, :], ACT.Sigmoid).then_inc(gate_sig, 1)
                    if m % 2:
                        center(2 + 3 * layer, m // 2)
                    if m >= 2 and layer + 1 < DEPTH:
                        copy_hT(3 + 3 * layer, 0, m - 2)

            for b in range(TB):
                copy_hT(0, 0, b)
            for layer in range(DEPTH):
                attention(layer, attn[layer])
                before_experts(layer)
                passes(act, layer, expert_group)
                embedding(layer)
            for m in range(4):
                b, j = divmod(m, 2)
                act.wait_ge(h_ready, 4 * (3 * DEPTH - 1) + m + 1)
                act.dma_start(out[0, b * P:(b + 1) * P, j * 512:(j + 1) * 512],
                              h[:, b, j * 512:(j + 1) * 512]).then_inc(out_sent, 16)

        @block.vector
        def _(dve):
            steps = [0]
            V = nc.vector

            def link(ins):
                steps[0] += 1
                ins.then_inc(vs, 1)
                dve.wait_ge(vs, steps[0])

            def stats_of(b, j):
                link(V.bn_stats(stats[:, b, j, :], acc[:, b, j * 512:(j + 1) * 512]))

            def layer_norm(n, b):
                mean, raw, dev, step, var, minus_half, minus_mean = (mv[:, b, i:i + 1] for i in range(7))
                link(V.bn_aggr(mv[:, b, 0:2], stats[:, b, :, :]))
                V.tensor_scalar(minus_mean, mean, -1.0, None, ALU.mult).then_inc(mean_ready, 1)
                link(V.tensor_scalar(var, raw, EPS, None, ALU.add))
                link(V.tensor_scalar(minus_half, var, -0.5, None, ALU.mult))
                link(V.tensor_scalar(step.bitcast(I32), var.bitcast(I32), 1, None, ALU.logical_shift_right))
                link(V.tensor_scalar(dev.bitcast(I32), step.bitcast(I32), -1.0, float(0x5F3759DF), ALU.mult, ALU.add))
                for _ in range(3):
                    link(V.scalar_tensor_tensor(step, dev, minus_half, dev, ALU.mult, ALU.mult))
                    link(V.scalar_tensor_tensor(dev, step, 1.5, dev, ALU.add, ALU.mult))
                dve.wait_ge(lnp_ready, 2 * n + 2)
                for j in range(2):
                    c = slice(j * 512, (j + 1) * 512)
                    dve.wait_ge(gained, 4 * n + 2 * b + j + 1)
                    V.scalar_tensor_tensor(h[:, b, c], h[:, b, c], dev, lnp[:, 1, c], ALU.mult, ALU.add).then_inc(h_ready, 1)

            def pick_keys():
                dve.wait_ge(idx_copied, 5)
                for b in range(TB):
                    for n in range(IDX_HEADS):
                        if b == 0:
                            dve.wait_ge(relued, n + 1)
                        before = causal[:, BLK[b]] if n == 0 else score[:, BLK[b]]
                        link(V.scalar_tensor_tensor(score[:, BLK[b]], relu[:, n, BLK[b]], iw[:, b, n:n + 1],
                                                    before, ALU.mult, ALU.add))
                for b in range(TB):
                    for _ in range(TOPK // 8):
                        link(V.max(top8, score[:, BLK[b]]))
                        link(V.match_replace(score[:, BLK[b]], top8, score[:, BLK[b]], TAKEN))
                link(V.tensor_scalar(pen, score, TAKEN, NEG, ALU.is_gt, ALU.mult))
                link(V.tensor_tensor(pen, pen, causal[:, :], ALU.add))

            def attention(layer, A):
                if layer == 0:
                    pick_keys()
                mask = pen if layer == 0 else causal[:, :]

                def softmax(n):
                    link(V.scalar_tensor_tensor(bias[:, n % 2, :], dist[:, :], 2.0 ** -(8 * (n + 1) / HEADS), mask,
                                                ALU.mult, ALU.add))
                    dve.wait_ge(A.qk, n + 1)
                    if n >= 2:
                        dve.wait_ge(A.p_turn, n - 1)
                    V.scalar_tensor_tensor(prob[:, n % 2, :], bank[4 + n % 2][:, 0:AW], SCALE, bias[:, n % 2, :],
                                           ALU.mult, ALU.add).then_inc(A.logits, 1)
                    dve.wait_ge(A.logits, n + 1)
                    for b in range(TB):
                        V.tensor_reduce(small[:, 2 * n + b:2 * n + b + 1], prob[:, n % 2, BLK[b]], AX_X, ALU.max,
                                        negate=True).then_inc(A.peak, 1)
                    dve.wait_ge(A.exps, 2 * n + 2)
                    link(V.reciprocal(small[:, 32:34], small[:, 16 + 2 * n:18 + 2 * n]))
                    for b in range(TB):
                        V.tensor_scalar(prob[:, n % 2, BLK[b]], prob[:, n % 2, BLK[b]], small[:, 32 + b:33 + b], None,
                                        ALU.mult).then_inc(A.normed, 1)
                    dve.wait_ge(A.normed, 2 * n + 2)

                for n in range(HEADS):
                    softmax(n)
                for b in range(TB):
                    for j in range(2):
                        if b == 0:
                            dve.wait_ge(mix_dot, 2 * layer + j + 1)
                        else:
                            dve.wait_ge(dense_used, W_O[layer] + j + 1)
                        link(V.scalar_tensor_tensor(acc[:, b, j * 512:(j + 1) * 512], h[:, b, j * 512:(j + 1) * 512],
                                                    ALPHA, bank[2 * b + j][:, :], ALU.mult, ALU.add))
                        stats_of(b, j)
                    layer_norm(3 * layer, b)

            def wide(a, shape):
                return a.broadcast_to(shape)

            SLOT_SHAPE = [P, TB, LANES, CAP]

            def of_group(a, g):
                return wide(a[:, :, bass.ds(g * LANES, LANES)].unsqueeze(3), SLOT_SHAPE)

            def pick_group(S, g):
                V.tensor_tensor(pick, wide(iota[:, :].unsqueeze(1).unsqueeze(1), SLOT_SHAPE), of_group(rank, g),
                                ALU.is_equal).then_inc(S.picked, 1)

            def router(layer):
                for b in range(TB):
                    g, e = lg[:, b, 0:NG], lg[:, b, NG:]
                    R, em_b, tmp, tmp2 = route[:, b, :], em[:, b, :], etmp[:, b, :], etmp2[:, b, :]
                    dve.wait_ge(router_dot, 2 * layer + b + 1)
                    link(V.tensor_copy(lg[:, b, :], bank[4 + 2 * b][:, 0:NG + NE]))
                    link(V.tensor_reduce(R[:, 8:9], g, AX_X, ALU.max))
                    V.tensor_reduce(R[:, 9:10], g, AX_X, ALU.max, negate=True).then_inc(r_exp_in, 1)
                    link(V.scalar_tensor_tensor(gpen[:, b, :], g, R[:, 8:9], rev[:, 0:NG], ALU.is_equal, ALU.mult))
                    link(V.tensor_reduce(R[:, 10:11], gpen[:, b, :], AX_X, ALU.max))
                    link(V.tensor_scalar(gpen[:, b, :], gpen[:, b, :], R[:, 10:11], NEG, ALU.not_equal, ALU.mult))
                    link(V.tensor_tensor(em_b.rearrange("p (g e) -> p g e", g=NG), e.rearrange("p (g e) -> p g e", g=NG),
                                         wide(gpen[:, b, :].unsqueeze(2), [P, NG, EPG]), ALU.add))
                    V.max(R[:, 0:8], em_b).then_inc(r_exp_in, 1)
                    dve.wait_ge(r_exp_in, 4 * layer + 2 * b + 2)
                    V.scalar_tensor_tensor(tmp2, em_b, R[:, 1:2], rev[:, :], ALU.is_equal, ALU.mult).then_inc(vs, 1)
                    steps[0] += 1
                    link(V.scalar_tensor_tensor(tmp, em_b, R[:, 0:1], rev[:, :], ALU.is_equal, ALU.mult))
                    link(V.tensor_reduce(R[:, 10:11], tmp, AX_X, ALU.max))
                    link(V.tensor_scalar(first[:, b, :], tmp, R[:, 10:11], None, ALU.is_equal))
                    link(V.scalar_tensor_tensor(tmp2, first[:, b, :], 0.0, tmp2, ALU.is_equal, ALU.mult))
                    link(V.tensor_reduce(R[:, 11:12], tmp2, AX_X, ALU.max))
                    V.scalar_tensor_tensor(assign[:, b, :], tmp2, R[:, 11:12], first[:, b, :], ALU.is_equal, ALU.add).then_inc(routed, 1)
                    V.tensor_scalar(second[:, b, :], tmp2, R[:, 11:12], None, ALU.is_equal).then_inc(vs, 1)
                    steps[0] += 1
                dve.wait_ge(ranked, 2 * layer + 1)
                dve.wait_ge(routed, TB * (layer + 1))
                link(V.scalar_tensor_tensor(rank[:, :, 0:NE], bank[5][:, 0:TB * NE].rearrange("p (b e) -> p b e", b=TB), 1.0,
                                            assign[:, :, :], ALU.add, ALU.mult))
                pick_group(main[layer], 0)
                dve.wait_ge(ranked, 2 * layer + 2)
                V.tensor_reduce(most[:, :], bank[7][:, 0:NE], AX_X, ALU.max).then_inc(max_ready, 1)
                dve.wait_ge(r_exp, 4 * layer + 2 * TB)
                full = [P, TB, NE]
                group_sum, second_exp, total, w1, w2 = (route[:, :, i:i + 1] for i in range(12, 17))
                link(V.scalar_tensor_tensor(total, second_exp, 1.0, group_sum, ALU.add, ALU.mult))
                link(V.reciprocal(w1, total))
                link(V.tensor_tensor(w2, w1, second_exp, ALU.mult))
                link(V.tensor_tensor(weight[:, :, :], first[:, :, :], wide(w1, full), ALU.mult))
                link(V.tensor_tensor(etmp[:, :, :], second[:, :, :], wide(w2, full), ALU.mult))
                link(V.tensor_tensor(weight[:, :, :], weight[:, :, :], etmp[:, :, :], ALU.add))

            def expert_group(S, n, g, turn, q, r):
                dve.wait_ge(S.picked, n + (r + 1))
                V.tensor_tensor(wpick, pick, of_group(weight, g), ALU.mult).then_inc(S.mid, 1)
                dve.wait_ge(S.sigmoid, n + 1)
                V.tensor_tensor(half, bank[2][:, :], sig, ALU.mult).then_inc(S.mid, 1)
                dve.wait_ge(S.wturn, n + 1)
                V.tensor_copy(pickT, bank[7][:, 0:T]).then_inc(S.pickT, 1)
                dve.wait_ge(S.mid, n * 3 + 2)
                up_done(dve, S, n)
                V.tensor_tensor(mid, half, bank[3][:, :], ALU.mult).then_inc(S.mid, 1)
                dve.wait_ge(S.gathered, n * GATE_CHUNKS + GATE_CHUNKS)
                pick_group(S, g + 1)
                dve.wait_ge(S.added, n * ADDS + TB)
                for k in range(4):
                    dve.wait_ge(S.comb, n * 4 + (k + 1))
                    a = acc[:, k // 2, (k % 2) * 512:(k % 2 + 1) * 512]
                    V.tensor_tensor(a, a, bank[k][:, :], ALU.add).then_inc(S.added, 1)
                    if k < 2:
                        dve.wait_ge(S.added, n * ADDS + (TB + 2 * k + 1))
                        V.bn_stats(stats[:, 0, k, :], a).then_inc(S.added, 1)

            def next_round(S, done, r):
                V.tensor_scalar(rank[:, :, 0:NE], rank[:, :, 0:NE], -float(CAP), None, ALU.add).then_inc(done, 1)
                dve.wait_ge(done, r + 1)
                pick_group(S, 0)

            link(V.memset(rank[:, :, NE:], 0.0))
            dve.wait_ge(consts_ready, 5)
            link(V.tensor_scalar(ident[:, :], dist[:, BLK[0]], 0.0, None, ALU.is_equal))
            link(V.tensor_scalar(tri[:, :], dist[:, BLK[0]], 0.0, None, ALU.is_gt))
            V.tensor_scalar(causal[:, :], dist[:, :], 0.0, NEG, ALU.is_gt, ALU.mult).then_inc(consts_ready, 1)
            dve.wait_ge(consts_ready, 6)
            for layer in range(DEPTH):
                attention(layer, attn[layer])
                router(layer)
                passes(dve, layer, expert_group, next_round)
                for b in range(TB):
                    if b:
                        for j in range(2):
                            stats_of(b, j)
                    layer_norm(3 * layer + 1, b)
                for b in range(TB):
                    for j in range(2):
                        m = 2 * b + j
                        dve.wait_ge(gate_sig, 4 * layer + m + 1)
                        if m < 3:
                            dve.wait_ge(ple_dot, 3 * layer + m + 1)
                        else:
                            dve.wait_ge(dense_used, W_PLE[layer] + 1)
                        link(V.tensor_tensor(gated[:, m, :], bank[m][:, :], gate[:, m, :], ALU.mult))
                        dve.wait_ge(h_ready, 4 * (3 * layer + 1) + m + 1)
                        link(V.scalar_tensor_tensor(acc[:, b, j * 512:(j + 1) * 512], h[:, b, j * 512:(j + 1) * 512],
                                                    ALPHA, gated[:, m, :], ALU.mult, ALU.add))
                        stats_of(b, j)
                    layer_norm(3 * layer + 2, b)

        @block.tensor
        def _(pe):
            mm, transpose = nc.tensor.matmul, nc.tensor.transpose

            def stay_warm(n, o):
                for _ in range(n):
                    mm(o[:, :], ident[:, :], h[:, 0, 0:512], start=True, stop=True)

            def turn(event, first_bank, b):
                for j in range(2):
                    if event == 0:
                        pe.wait_ge(x_in[b], 16)
                    else:
                        pe.wait_ge(h_ready, 4 * (event - 1) + 2 * b + j + 1)
                    for k in range(4):
                        ins = transpose(bank[first_bank + 2 * b + j][:, k * P:(k + 1) * P],
                                        h[:, b, (4 * j + k) * P:(4 * j + k + 1) * P], ident[:, :])
                    ins.then_inc(turned, 1)

            def turned_here(event, b, j=1):
                pe.wait_ge(hT_ready, 4 * event + 2 * b + j + 1)

            def columns(o, w, c0, n, tokens=slice(0, T)):
                for k in range(KC):
                    ins = mm(o, w[:, k, c0:c0 + n], hT[:, k, tokens], start=(k == 0), stop=(k == KC - 1))
                return ins

            def rows(o, w, b, c0, n, event=None):
                for k in range(KC):
                    if event is not None and k % 4 == 0:
                        turned_here(event, b, k // 4)
                    ins = mm(o, hT[:, k, b * P:(b + 1) * P], w[:, k, c0:c0 + n], start=(k == 0), stop=(k == KC - 1))
                return ins

            def index_projections():
                dense_here(pe, A_IDX)
                w = dense_slot(A_IDX)
                for n in range(2):
                    columns(bank[4][:, n * T:(n + 1) * T], w, n * P, P)
                columns(bank[5][0:IDX_DIM + IDX_HEADS, 0:T], w, IK0 - IQ0, IDX_DIM + IDX_HEADS).then_inc(dense_used, 1)

            def index_products():
                pe.wait_ge(idx_copied, 4)
                part = slice(IDX_DIM, IDX_DIM + IDX_HEADS)
                for b in range(TB):
                    ins = transpose(bank[5][:, b * IDX_HEADS:(b + 1) * IDX_HEADS], iwT[:, b * P:(b + 1) * P], ident[part, part])
                ins.then_inc(iw_turned, 1)
                for n in range(0, IDX_HEADS, 2):
                    for b in range(TB):
                        for i in range(2):
                            part = slice(IDX_DIM * i, IDX_DIM * (i + 1))
                            ins = mm(bank[n + i][:, BLK[b]], iqT[part, n // 2, b * P:(b + 1) * P],
                                     ikT[part, 0:P * (b + 1)], start=True, stop=True)
                    ins.then_inc(rel_dot, 1)

            def turn_p():
                pe.wait_ge(p_in, 16 * DEPTH)
                pe.wait_ge(idx_copied, 5)
                for layer in range(DEPTH):
                    for k in range(PC):
                        for b in range(TB):
                            ins = transpose(bank[4 + layer][:, k * T + b * P:k * T + (b + 1) * P],
                                            psb[:, layer, b, k * P:(k + 1) * P], ident[:, :])
                    ins.then_inc(p_turned, 1)

            def attention(layer, A, event):
                if layer == 0:
                    for b in range(TB):
                        turned_here(event, b)
                    index_projections()
                else:
                    pe.wait_ge(gate_sig, 4 * (layer - 1) + 2)
                j = W_KV[layer]
                dense_here(pe, j)
                w = dense_slot(j)

                def queries_of_block_0(n):
                    dense_here(pe, W_Q[layer])
                    columns(bank[n][:, 0:P], dense_slot(W_Q[layer]), n * P, P, slice(0, P))

                for b in range(TB):
                    tokens = slice(b * P, (b + 1) * P)
                    turned_here(event, b)
                    for n in range(KV_HEADS):
                        ins = columns(bank[K_BANK[layer]][:, n * T + b * P:n * T + (b + 1) * P], w, n * P, P, tokens)
                    if b == TB - 1:
                        ins.then_inc(A.k_dot, 1)
                    elif layer == 0:
                        index_products()
                    ins = rows(bank[K_BANK[layer] + 1][:, b * KV:(b + 1) * KV], w, b, KV, KV)
                    if layer and b == 0:
                        queries_of_block_0(0)
                        turn(event, 0, 1)
                        queries_of_block_0(1)
                ins.then_inc(dense_used, 1)
                if layer == 0:
                    turn_p()
                    pe.wait_ge(relued, IDX_HEADS)

                def project_q(n):
                    j = W_Q[layer] + n // 4
                    if n % 4 == 0:
                        dense_here(pe, j)
                    if n >= 4:
                        pe.wait_ge(A.q_copied, n - 3)
                    if layer and n < 2:
                        ins = columns(bank[n][:, P:T], dense_slot(j), n * P, P, slice(P, T))
                    else:
                        ins = columns(bank[n % 4][:, 0:T], dense_slot(j), (n % 4) * P, P)
                    ins.then_inc(dense_used if n % 4 == 3 else A.q_dot, 1)

                def qk(n):
                    pe.wait_ge(A.q_copied, n + 1)
                    if n >= 2:
                        pe.wait_ge(A.logits, n - 1)
                    for b in range(TB):
                        ins = mm(bank[4 + n % 2][:, BLK[b]], qT[:, n, b * P:(b + 1) * P],
                                 kT[:, n // GROUP, 0:P * (b + 1)], start=True, stop=True)
                    ins.then_inc(A.qk, 1)

                def turn_prob(n):
                    pe.wait_ge(A.normed, 2 * n + 2)
                    if n:
                        pe.wait_ge(A.probT_ready, n)
                    for k in range(3):
                        ins = transpose(bank[6][:, k * P:(k + 1) * P], prob[:, n % 2, k * P:(k + 1) * P], ident[:, :])
                    ins.then_inc(A.p_turn, 1)

                def pv(n):
                    pe.wait_ge(A.probT_ready, n + 1)
                    if n:
                        pe.wait_ge(A.o_copied, n)
                    o, hd = bank[7], slice(n // GROUP * HD, (n // GROUP + 1) * HD)
                    mm(o[:, 0:T], v[:, 0, hd], probT[:, 0:T], start=True, stop=False)
                    mm(o[:, P:T], v[:, 1, hd], probT[:, T:AW], start=False, stop=True).then_inc(A.pv, 1)

                def mix(m, heads):
                    b, half_ = divmod(m, 2)
                    dense_here(pe, W_O[layer] + half_)
                    for n in heads:
                        pe.wait_ge(A.o_copied, n + 1)
                        ins = mm(bank[m][:, :], qT[:, n, b * P:(b + 1) * P], dense_slot(W_O[layer] + half_)[:, n, :],
                                 start=(n == 0), stop=(n == HEADS - 1))
                    return ins

                for n in range(4):
                    project_q(n)
                    if n == 1:
                        pe.wait_ge(A.kv_copied, 2)
                        if layer == 0:
                            pe.wait_ge(pT_ready, DEPTH)
                        qk(0)
                for n in range(HEADS):
                    if n + 1 < HEADS:
                        qk(n + 1)
                    else:
                        mix(0, [4])
                    if n:
                        pv(n - 1)
                    if n < 4:
                        project_q(4 + n)
                    else:
                        pe.wait_ge(A.q_copied, n + 1)
                        mix(n - 4, range(4))
                    turn_prob(n)
                mix(1, [4])
                pv(HEADS - 1)
                for m in range(4):
                    mix(m, range(5 if m < 2 else 4, HEADS)).then_inc((mix_dot, dense_used)[m // 2], 1)

            def router(layer, event):
                for b in range(TB):
                    turn(event, 0, b)
                    o = bank[4 + 2 * b][:, 0:NG + NE]
                    for k in range(KC):
                        if k % 4 == 0:
                            turned_here(event, b, k // 4)
                        mm(o, hT[:, k, b * P:(b + 1) * P], wr[:, layer, k, :], start=(k == 0), stop=False)
                    mm(o, ones[0:1, :], brow[0:1, layer, :], start=False, stop=True).then_inc(router_dot, 1)
                    if b == 0:
                        stay_warm(2, bank[5])
                stay_warm(4, bank[3])
                ahead0, ahead1 = (bank[5][:, i * NE:(i + 1) * NE] for i in range(TB))
                total = bank[7][:, 0:NE]
                pe.wait_ge(routed, TB * layer + 1)
                mm(ahead0, tri[:, :], assign[:, 0, :], start=True, stop=True)
                mm(ahead1, ones[:, :], assign[:, 0, :], start=True, stop=False)
                pe.wait_ge(routed, TB * layer + 2)
                mm(ahead1, tri[:, :], assign[:, 1, :], start=False, stop=True).then_inc(ranked, 1)
                for b in range(TB):
                    ins = mm(total, ones[:, :], assign[:, b, :], start=(b == 0), stop=(b == TB - 1))
                ins.then_inc(ranked, 1)
                stay_warm(1, bank[3])

            def expert_group(S, n, g, turn, q, r):
                pe.wait_ge(S.picked, n + (r + 1))
                pe.wait_ge(S.added, n * ADDS + TB)

                def gather(c):
                    for i in range(2):
                        part = h[:, :, c * 2 * P:(c + 1) * 2 * P].rearrange("p b (d r) -> p b r d", r=2)
                        for b in range(TB):
                            ins = mm(gather_bank(c)[:, i * P:(i + 1) * P], part[:, b, i, :],
                                     pick[:, b].rearrange("p e s -> p (e s)"), start=(b == 0), stop=(b == TB - 1))
                    ins.then_inc(S.gathered, 1)

                def product(o, c, chunk):
                    expert_here(pe, S, turn, chunk)
                    for i in range(2):
                        for e in range(LANES):
                            lane = slice(e * CAP, (e + 1) * CAP)
                            ins = mm(o[lane, :], xgT[:, 2 * c + i, lane], expert_slot(chunk)[:, e, i, :],
                                     start=(c + i == 0), stop=(c == GATE_CHUNKS - 1 and i == 1))
                    ins.then_inc(S.used, 1)

                gather(0)
                for c in range(GATE_CHUNKS):
                    pe.wait_ge(S.xg, n * GATE_CHUNKS + (c + 1))
                    if c == 1:
                        gather(3)
                    product(bank[2], c, q * GCH + c)
                    if c == 0:
                        gather(1)
                        gather(2)
                pe.wait_ge(S.mid, n * 3 + 1)
                for b in range(TB):
                    ins = transpose(bank[7][:, b * P:(b + 1) * P], wpick[:, b].rearrange("p e s -> p (e s)"), ident[:, :])
                ins.then_inc(S.wturn, 1)
                for c in range(GATE_CHUNKS):
                    product(bank[3], c, q * GCH + GATE_CHUNKS + c)
                c = q * GCH + 2 * GATE_CHUNKS
                pe.wait_ge(S.mid, n * 3 + 3)
                for k in range(DOWN_CHUNKS):
                    ins = transpose(bank[6][:, k * P:(k + 1) * P], mid[:, k * P:(k + 1) * P], ident[:, :])
                ins.then_inc(S.mturn, 1)
                pe.wait_ge(S.midT, n + 1)
                for k in range(DOWN_CHUNKS):
                    if k == DOWN_CHUNKS - 1:
                        stay_warm(2, bank[3])
                    expert_here(pe, S, turn, c)
                    for half_ in range(2):
                        for e in range(LANES):
                            lane = slice(e * CAP, (e + 1) * CAP)
                            ins = mm(bank[4 + half_][lane, :], midT[:, k, lane],
                                     expert_slot(c)[:, e, half_ * 512:(half_ + 1) * 512],
                                     start=(k == 0), stop=(k == DOWN_CHUNKS - 1))
                        if k == DOWN_CHUNKS - 1 and half_ == 0:
                            ins.then_inc(S.down_half, 1)
                    ins.then_inc(S.used, 1)
                    c += 1
                pe.wait_ge(S.pickT, n + 1)
                for k in range(4):
                    b, half_ = k // 2, k % 2
                    if k < 2:
                        pe.wait_ge(S.y, n * 2 + (k + 1))
                    mm(bank[k][:, :], pickT[:, b * P:(b + 1) * P], y[:, half_ * 512:(half_ + 1) * 512],
                       start=True, stop=True).then_inc(S.comb, 1)

            pe.wait_ge(consts_ready, 6)
            for b in range(TB):
                turn(0, 0, b)
            stay_warm(1, bank[4])
            for layer in range(DEPTH):
                event = 3 * layer
                attention(layer, attn[layer], event)
                pe.wait_ge(small_in, 32)
                router(layer, event + 1)
                passes(pe, layer, expert_group)
                dense_here(pe, W_PLE[layer])
                for m in range(4):
                    b, j = divmod(m, 2)
                    if m == 3:
                        turn(event + 2, 4, 0)
                    pe.wait_ge(main[layer].added, TB + ADDS * (NGRP - 1) + (2 * m + 1 if m < 2 else m + 3))
                    for c in range(PC):
                        ins = mm(bank[m][:, :], pT[:, layer, c, b * P:(b + 1) * P],
                                 dense_slot(W_PLE[layer])[:, c, j * 512:(j + 1) * 512], start=(c == 0), stop=(c == PC - 1))
                    ins.then_inc(ple_dot if m < 3 else dense_used, 1)
                for b in range(TB):
                    for j in range(2):
                        if b and j and layer + 1 < DEPTH:
                            turn(event + 3, 0, 0)
                        dense_here(pe, W_PLE[layer] + 1 + j)
                        rows(bank[4 + 2 * b + j][:, :], dense_slot(W_PLE[layer] + 1 + j), b, 0, 512,
                             event + 2)\
                            .then_inc((gate_dot, dense_used)[b], 1)
                        if b == 0 and j == 0:
                            turn(event + 2, 4, 1)


INPUTS = ["x", "p", "w_in_a", "w_o_a", "w_kv_shared", "w_q_b", "w_o_b", "w_router", "b_router", "w_gate", "w_up", "w_down", "w_ple", "w_ple_gate", "ln_g", "ln_b"]


def kernel(**inputs):
    import numpy as np
    import concourse.bacc as bacc
    from concourse.bass_utils import run_bass_kernel_spmd

    nc = bacc.Bacc("TRN2", target_bir_lowering=False, num_devices=1)
    w = np.concatenate([inputs["w_router_group"], inputs["w_router_expert"]], axis=2)
    inputs["w_router"] = w.reshape(DEPTH, KC, P, NG + NE).transpose(2, 0, 1, 3)
    inputs["b_router"] = np.concatenate([inputs["b_router_group"], inputs["b_router_expert"]], axis=1)[None]
    arrays, args = {}, []
    for name in INPUTS:
        a = np.ascontiguousarray(inputs[name])
        arrays[f"in_{name}"] = a
        args.append(nc.dram_tensor(f"in_{name}", a.shape, mybir.dt.from_np(a.dtype), kind="ExternalInput").ap())
    args.append(nc.dram_tensor("out_h", (1, T, D), F32, kind="ExternalOutput").ap())
    trunk(nc, *args)
    r = run_bass_kernel_spmd(nc, [arrays], core_ids=[0])
    return r.results[0]["out_h"]
```
